# Optimizing a Trainium2 kernel written in Bass

```python
import math
import jax, jax.numpy as jnp
from jax import lax
import numpy as np

D_MODEL = 1024
BATCH = 1
SEQ = 512
DEPTH = 2

NORM_EPS = 1e-6
D_FF = 2816
D_MIX = D_MODEL
MLA_HEADS = 8
MLA_NOPE_DIM = 64
MLA_ROPE_DIM = 32
MLA_V_DIM = 64
MLA_QK_DIM = MLA_NOPE_DIM + MLA_ROPE_DIM
MLA_Q_RANK = 256
MLA_KV_RANK = 128
MLA_WIDTH = MLA_HEADS * MLA_V_DIM
ROPE_THETA = 10000.0
Q_BLOCK = 128
CONV_WIDTH = D_MIX // 4
CONV_KERNEL = 31
HY_WIDTH = D_MIX - MLA_WIDTH - CONV_WIDTH
HY_ORDER = 2
HY_SHORT_KERNEL = 3
HY_EMB_DIM = 33
HY_FILTER_DIM = 64
HY_FAST_DECAY_PCT = 0.3
HY_SLOW_DECAY_PCT = 1.5
HY_DECAY_TARGET = 1e-2
HY_FILTER_OUT = HY_ORDER * 2 * HY_WIDTH
IN_MLA_Q = MLA_Q_RANK
IN_MLA_KV = MLA_KV_RANK
IN_MLA_KPE = MLA_ROPE_DIM
IN_CONV = 2 * CONV_WIDTH
IN_HY = (HY_ORDER + 1) * HY_WIDTH
OFF_Q = 0
OFF_KV = OFF_Q + IN_MLA_Q
OFF_KPE = OFF_KV + IN_MLA_KV
OFF_CONV = OFF_KPE + IN_MLA_KPE
OFF_HY = OFF_CONV + IN_CONV
IN_COLS = OFF_HY + IN_HY


def rmsnorm(x, g):
    xf = x.astype(jnp.float32)
    xf = xf * lax.rsqrt(jnp.mean(xf * xf, axis=-1, keepdims=True) + NORM_EPS)
    return (xf * g.astype(jnp.float32)).astype(x.dtype)

def layernorm(x, g, b):
    xf = x.astype(jnp.float32)
    mu = jnp.mean(xf, axis=-1, keepdims=True)
    var = jnp.mean(jnp.square(xf - mu), axis=-1, keepdims=True)
    y = (xf - mu) * lax.rsqrt(var + NORM_EPS)
    return (y * g.astype(jnp.float32) + b.astype(jnp.float32)).astype(x.dtype)

def swiglu(h, w_gate, w_up, w_down):
    return (jax.nn.silu(h @ w_gate) * (h @ w_up)) @ w_down

def depthwise_conv(u, w, b):
    k, c = w.shape
    pad = k // 2
    y = lax.conv_general_dilated(u, w[:, None, :].astype(u.dtype), window_strides=(1,),
                                 padding=[(pad, pad)], dimension_numbers=('NWC', 'WIO', 'NWC'),
                                 feature_group_count=c)
    return y + b.astype(u.dtype)

def rope_cos_sin(positions, dtype):
    inv_freq = 1.0 / (ROPE_THETA ** (jnp.arange(0, MLA_ROPE_DIM, 2, dtype=jnp.float32) / MLA_ROPE_DIM))
    ang = positions.astype(jnp.float32)[..., None] * inv_freq
    return jnp.cos(ang).astype(dtype), jnp.sin(ang).astype(dtype)

def apply_rope(x, cos, sin):
    x1, x2 = jnp.split(x, 2, axis=-1)
    return jnp.concatenate([x1 * cos - x2 * sin, x1 * sin + x2 * cos], axis=-1)

def mla_mixer(h_q, h_kv, k_pe, positions, q_norm, w_qb, kv_norm, w_kvb):
    b, l, _ = h_q.shape
    cos, sin = rope_cos_sin(positions, h_q.dtype)
    q = (rmsnorm(h_q, q_norm) @ w_qb).reshape(b, l, MLA_HEADS, MLA_QK_DIM)
    q_pe = apply_rope(q[..., MLA_NOPE_DIM:], cos[:, :, None], sin[:, :, None])
    q = jnp.concatenate([q[..., :MLA_NOPE_DIM], q_pe], axis=-1) * (MLA_QK_DIM ** -0.5)
    kv = (rmsnorm(h_kv, kv_norm) @ w_kvb).reshape(b, l, MLA_HEADS, MLA_NOPE_DIM + MLA_V_DIM)
    k_pe = apply_rope(k_pe, cos, sin)
    k = jnp.concatenate([kv[..., :MLA_NOPE_DIM],
                         jnp.broadcast_to(k_pe[:, :, None], (b, l, MLA_HEADS, MLA_ROPE_DIM))], axis=-1)
    v = kv[..., MLA_NOPE_DIM:]
    n_blk = l // Q_BLOCK
    q_blocks = q.reshape(b, n_blk, Q_BLOCK, MLA_HEADS, MLA_QK_DIM).transpose(1, 0, 2, 3, 4)

    def attend(qb):
        s = jnp.einsum('bqhd,bkhd->bhqk', qb, k).astype(jnp.float32)
        p = jax.nn.softmax(s, axis=-1).astype(v.dtype)
        return jnp.einsum('bhqk,bkhd->bqhd', p, v)

    o = lax.map(attend, q_blocks)
    return o.transpose(1, 0, 2, 3, 4).reshape(b, l, MLA_WIDTH)

def conformer_conv_mixer(h_conv, dw_w, dw_b, ln_g, ln_b):
    a, g = jnp.split(h_conv, 2, axis=-1)
    u = a * jax.nn.sigmoid(g)
    u = depthwise_conv(u, dw_w, dw_b)
    return jax.nn.silu(layernorm(u, ln_g, ln_b))

def hyena_filters(l, w1, b1, w2, b2, w3, b3, w4, freq):
    f32 = jnp.float32
    t = jnp.linspace(0.0, 1.0, l, dtype=f32)[:, None]
    bands = (HY_EMB_DIM - 1) // 2
    ang = 2.0 * math.pi * jnp.arange(l, dtype=f32)[:, None] / l
    fb = jnp.linspace(1e-4, bands - 1, bands, dtype=f32)[None, :]
    z = jnp.concatenate([t, jnp.cos(fb * ang), -jnp.sin(fb * ang)], axis=-1)
    fr = freq.astype(f32)
    hdn = jnp.sin(fr * (z @ w1.astype(f32) + b1.astype(f32)))
    hdn = jnp.sin(fr * (hdn @ w2.astype(f32) + b2.astype(f32)))
    hdn = jnp.sin(fr * (hdn @ w3.astype(f32) + b3.astype(f32)))
    h = (hdn @ w4.astype(f32)).reshape(l, HY_ORDER, 2, HY_WIDTH)
    max_decay = math.log(HY_DECAY_TARGET) / HY_FAST_DECAY_PCT
    min_decay = math.log(HY_DECAY_TARGET) / HY_SLOW_DECAY_PCT
    deltas = jnp.linspace(min_decay, max_decay, HY_WIDTH, dtype=f32)
    h = h * jnp.exp(-t * jnp.abs(deltas))[:, None, None, :]
    fwd, bwd = h[:, :, 0], h[:, :, 1]
    k = jnp.concatenate([fwd, jnp.zeros_like(fwd[:1]), jnp.flip(bwd[1:], axis=0)], axis=0)
    return k / jnp.sum(jnp.abs(k), axis=0, keepdims=True)

def fft_long_conv(u, k, d):
    l = u.shape[1]
    uf = u.astype(jnp.float32)
    uk = jnp.fft.rfft(uf, n=2 * l, axis=1) * jnp.fft.rfft(k, axis=0)[None]
    y = jnp.fft.irfft(uk, n=2 * l, axis=1)[:, :l]
    return (y + uf * d.astype(jnp.float32)).astype(u.dtype)

def hyena_mixer(h_hy, short_w, short_b, w1, b1, w2, b2, w3, b3, w4, freq, bias_d):
    u = depthwise_conv(h_hy, short_w, short_b)
    v, x1, x2 = jnp.split(u, HY_ORDER + 1, axis=-1)
    k = hyena_filters(h_hy.shape[1], w1, b1, w2, b2, w3, b3, w4, freq)
    z = x1 * fft_long_conv(v, k[:, 0], bias_d[0])
    return x2 * fft_long_conv(z, k[:, 1], bias_d[1])

def first_inputs(seed: int = 0) -> dict:
    key = jax.random.key(seed)
    ks = iter(jax.random.split(key, 64))
    f32 = jnp.float32

    def nrm(shape, scale):
        return jax.random.normal(next(ks), shape, f32) * scale

    def gain(shape):
        return 1.0 + nrm(shape, 0.05)

    dd = DEPTH
    return {
        "x": nrm((BATCH, SEQ, D_MODEL), 1.0),
        "positions": jnp.broadcast_to(jnp.arange(SEQ, dtype=jnp.int32)[None], (BATCH, SEQ)),
        "ffn1_norm": gain((dd, D_MODEL)),
        "ffn1_w_gate": nrm((dd, D_MODEL, D_FF), D_MODEL ** -0.5),
        "ffn1_w_up": nrm((dd, D_MODEL, D_FF), D_MODEL ** -0.5),
        "ffn1_w_down": nrm((dd, D_FF, D_MODEL), D_FF ** -0.5),
        "mix_norm": gain((dd, D_MODEL)),
        "w_in": nrm((dd, D_MODEL, IN_COLS), D_MODEL ** -0.5),
        "mla_q_norm": gain((dd, MLA_Q_RANK)),
        "mla_w_qb": nrm((dd, MLA_Q_RANK, MLA_HEADS * MLA_QK_DIM), MLA_Q_RANK ** -0.5),
        "mla_kv_norm": gain((dd, MLA_KV_RANK)),
        "mla_w_kvb": nrm((dd, MLA_KV_RANK, MLA_HEADS * (MLA_NOPE_DIM + MLA_V_DIM)), MLA_KV_RANK ** -0.5),
        "conv_dw_w": nrm((dd, CONV_KERNEL, CONV_WIDTH), CONV_KERNEL ** -0.5),
        "conv_dw_b": nrm((dd, CONV_WIDTH), 0.02),
        "conv_ln_g": gain((dd, CONV_WIDTH)),
        "conv_ln_b": nrm((dd, CONV_WIDTH), 0.02),
        "hy_short_w": nrm((dd, HY_SHORT_KERNEL, IN_HY), HY_SHORT_KERNEL ** -0.5),
        "hy_short_b": nrm((dd, IN_HY), 0.02),
        "hy_filt_w1": nrm((dd, HY_EMB_DIM, HY_FILTER_DIM), HY_EMB_DIM ** -0.5),
        "hy_filt_b1": nrm((dd, HY_FILTER_DIM), 0.1),
        "hy_filt_w2": nrm((dd, HY_FILTER_DIM, HY_FILTER_DIM), HY_FILTER_DIM ** -0.5),
        "hy_filt_b2": nrm((dd, HY_FILTER_DIM), 0.1),
        "hy_filt_w3": nrm((dd, HY_FILTER_DIM, HY_FILTER_DIM), HY_FILTER_DIM ** -0.5),
        "hy_filt_b3": nrm((dd, HY_FILTER_DIM), 0.1),
        "hy_filt_w4": nrm((dd, HY_FILTER_DIM, HY_FILTER_OUT), HY_FILTER_DIM ** -0.5),
        "hy_filt_freq": gain((dd, HY_FILTER_DIM)),
        "hy_bias_d": nrm((dd, HY_ORDER, HY_WIDTH), 0.5),
        "out_norm": gain((dd, D_MIX)),
        "w_out": nrm((dd, D_MIX, D_MODEL), D_MIX ** -0.5),
        "ffn2_norm": gain((dd, D_MODEL)),
        "ffn2_w_gate": nrm((dd, D_MODEL, D_FF), D_MODEL ** -0.5),
        "ffn2_w_up": nrm((dd, D_MODEL, D_FF), D_MODEL ** -0.5),
        "ffn2_w_down": nrm((dd, D_FF, D_MODEL), D_FF ** -0.5),
        "final_norm": gain((D_MODEL,)),
    }

def first_block(x, positions, ffn1_norm, ffn1_w_gate, ffn1_w_up, ffn1_w_down, mix_norm, w_in,
              mla_q_norm, mla_w_qb, mla_kv_norm, mla_w_kvb, conv_dw_w, conv_dw_b, conv_ln_g, conv_ln_b,
              hy_short_w, hy_short_b, hy_filt_w1, hy_filt_b1, hy_filt_w2, hy_filt_b2, hy_filt_w3, hy_filt_b3,
              hy_filt_w4, hy_filt_freq, hy_bias_d, out_norm, w_out, ffn2_norm, ffn2_w_gate, ffn2_w_up,
              ffn2_w_down, final_norm):
    e1 = MLA_WIDTH
    e2 = MLA_WIDTH + CONV_WIDTH
    for i in range(DEPTH):
        x = x + 0.5 * swiglu(rmsnorm(x, ffn1_norm[i]), ffn1_w_gate[i], ffn1_w_up[i], ffn1_w_down[i])
        h = rmsnorm(x, mix_norm[i]) @ w_in[i]
        y_mla = mla_mixer(h[..., OFF_Q:OFF_KV], h[..., OFF_KV:OFF_KPE], h[..., OFF_KPE:OFF_CONV], positions,
                          mla_q_norm[i], mla_w_qb[i], mla_kv_norm[i], mla_w_kvb[i])
        y_conv = conformer_conv_mixer(h[..., OFF_CONV:OFF_HY], conv_dw_w[i], conv_dw_b[i],
                                      conv_ln_g[i], conv_ln_b[i])
        y_hy = hyena_mixer(h[..., OFF_HY:], hy_short_w[i], hy_short_b[i], hy_filt_w1[i], hy_filt_b1[i],
                           hy_filt_w2[i], hy_filt_b2[i], hy_filt_w3[i], hy_filt_b3[i], hy_filt_w4[i],
                           hy_filt_freq[i], hy_bias_d[i])
        g = out_norm[i]
        y = jnp.concatenate([rmsnorm(y_mla, g[:e1]), rmsnorm(y_conv, g[e1:e2]), rmsnorm(y_hy, g[e2:])], axis=-1)
        x = x + y @ w_out[i]
        x = x + 0.5 * swiglu(rmsnorm(x, ffn2_norm[i]), ffn2_w_gate[i], ffn2_w_up[i], ffn2_w_down[i])
    return rmsnorm(x, final_norm)


DEPTH_2 = 1

SSM_EXPAND = 2
SSM_D_INNER = SSM_EXPAND * D_MODEL
SSM_HEAD_DIM = 64
SSM_N_HEADS = SSM_D_INNER // SSM_HEAD_DIM
SSM_N_GROUPS = 4
SSM_D_STATE = 128
SSM_CONV = 4
SSM_CHUNK = 128
SSM_CONV_DIM = SSM_D_INNER + 2 * SSM_N_GROUPS * SSM_D_STATE

ATT_HEAD_DIM = 128
ATT_HEADS_PER_GROUP = 4
ATT_PATTERNS = ((128, 1), (512, 4), (2048, 16))
ATT_N_HEADS = ATT_HEADS_PER_GROUP * len(ATT_PATTERNS)
ATT_QKV_DIM = 3 * ATT_N_HEADS * ATT_HEAD_DIM
ATT_OUT_DIM = ATT_HEADS_PER_GROUP * ATT_HEAD_DIM
ATT_BLOCK = 128

N_BRANCH = 2
D_FF_2 = -(-8 * D_MODEL // (3 * 256)) * 256
IN_PROJ_SIZES = (SSM_D_INNER, SSM_CONV_DIM, SSM_N_HEADS, ATT_QKV_DIM, N_BRANCH * D_MODEL)
IN_PROJ_DIM = sum(IN_PROJ_SIZES)
EPS = 1e-6


def rmsnorm_2(x, g):
    xf = x.astype(jnp.float32)
    y = xf * lax.rsqrt(jnp.mean(xf * xf, axis=-1, keepdims=True) + EPS)
    return (y * g.astype(jnp.float32)).astype(x.dtype)

def rope(t, pos):
    half = t.shape[-1] // 2
    inv = ROPE_THETA ** (-jnp.arange(half, dtype=jnp.float32) / half)
    ang = pos.astype(jnp.float32)[:, None] * inv[None, :]
    cos = jnp.cos(ang)[None, :, None, :]
    sin = jnp.sin(ang)[None, :, None, :]
    t1, t2 = t[..., :half], t[..., half:]
    return jnp.concatenate([t1 * cos - t2 * sin, t2 * cos + t1 * sin], axis=-1)

def segsum(a):
    T = a.shape[-1]
    xx = jnp.broadcast_to(a[..., :, None], a.shape + (T,))
    cs = jnp.cumsum(jnp.where(jnp.tril(jnp.ones((T, T), bool), -1), xx, 0.0), axis=-2)
    return jnp.where(jnp.tril(jnp.ones((T, T), bool)), cs, -jnp.inf)

def causal_depthwise_conv(u, w, b):
    K, C = w.shape
    out = lax.conv_general_dilated(u, w[:, None, :], window_strides=(1,), padding=[(K - 1, 0)],
                                   dimension_numbers=('NWC', 'WIO', 'NWC'), feature_group_count=C)
    return out + b

def ssd_chunked(xs, dt, A, Bm, Cm):
    b, S, H, P = xs.shape
    G, N = Bm.shape[-2:]
    J = H // G
    Q = SSM_CHUNK
    nc = S // Q
    xdt = (xs * dt[..., None]).reshape(b, nc, Q, G, J, P)
    a = (dt * A).reshape(b, nc, Q, G, J).transpose(0, 1, 3, 4, 2)
    a_cs = jnp.cumsum(a, axis=-1)
    Br = Bm.reshape(b, nc, Q, G, N)
    Cr = Cm.reshape(b, nc, Q, G, N)
    tri = jnp.tril(jnp.ones((Q, Q), bool))
    Lmat = jnp.exp(jnp.where(tri, a_cs[..., :, None] - a_cs[..., None, :], -jnp.inf))
    CB = jnp.einsum('bclgn,bcsgn->bcgls', Cr, Br)
    y_diag = jnp.einsum('bcgjls,bcsgjp->bclgjp', CB[:, :, :, None] * Lmat, xdt)
    decay_states = jnp.exp(a_cs[..., -1:] - a_cs)
    states = jnp.einsum('bclgn,bcgjl,bclgjp->bcgjpn', Br, decay_states, xdt)
    chunk_tot = jnp.pad(a_cs[..., -1].transpose(0, 2, 3, 1), ((0, 0), (0, 0), (0, 0), (1, 0)))
    decay_chunk = jnp.exp(segsum(chunk_tot))
    states = jnp.concatenate([jnp.zeros_like(states[:, :1]), states], axis=1)
    new_states = jnp.einsum('bgjzc,bcgjpn->bzgjpn', decay_chunk, states)
    prev_states = new_states[:, :-1]
    y_off = jnp.einsum('bclgn,bcgjpn,bcgjl->bclgjp', Cr, prev_states, jnp.exp(a_cs))
    return (y_diag + y_off).reshape(b, S, H, P)

def mamba2_branch(z, xBC, dt_raw, conv_w, conv_b, dt_bias, a_log, d_skip, ssm_norm):
    b, S, _ = z.shape
    xBC = jax.nn.silu(causal_depthwise_conv(xBC, conv_w, conv_b)).astype(jnp.float32)
    gn = SSM_N_GROUPS * SSM_D_STATE
    xs = xBC[..., :SSM_D_INNER].reshape(b, S, SSM_N_HEADS, SSM_HEAD_DIM)
    Bm = xBC[..., SSM_D_INNER:SSM_D_INNER + gn].reshape(b, S, SSM_N_GROUPS, SSM_D_STATE)
    Cm = xBC[..., SSM_D_INNER + gn:].reshape(b, S, SSM_N_GROUPS, SSM_D_STATE)
    dt = jax.nn.softplus(dt_raw.astype(jnp.float32) + dt_bias.astype(jnp.float32))
    A = -jnp.exp(a_log.astype(jnp.float32))
    y = ssd_chunked(xs, dt, A, Bm, Cm) + d_skip.astype(jnp.float32)[:, None] * xs
    y = y.reshape(b, S, SSM_D_INNER) * jax.nn.silu(z.astype(jnp.float32))
    yg = y.reshape(b, S, SSM_N_GROUPS, SSM_D_INNER // SSM_N_GROUPS)
    yg = yg * lax.rsqrt(jnp.mean(yg * yg, axis=-1, keepdims=True) + EPS)
    y = yg.reshape(b, S, SSM_D_INNER) * ssm_norm.astype(jnp.float32)
    return y.astype(z.dtype)

def dilated_window_group(q, k, v, window, dilation):
    b, S, h, d = q.shape
    r = dilation
    w_sub = window // r
    L = S // r
    nb = -(-L // ATT_BLOCK)
    Lp = nb * ATT_BLOCK

    def to_blocks(t):
        t = t.reshape(b, L, r, h, d).transpose(0, 2, 1, 3, 4)
        t = jnp.pad(t, ((0, 0), (0, 0), (0, Lp - L), (0, 0), (0, 0)))
        return t.reshape(b, r, nb, ATT_BLOCK, h, d)

    def with_prev(t):
        prev = jnp.pad(t[:, :, :-1], ((0, 0), (0, 0), (1, 0), (0, 0), (0, 0), (0, 0)))
        return jnp.concatenate([prev, t], axis=3)

    qb = to_blocks(q)
    kk = with_prev(to_blocks(k))
    vv = with_prev(to_blocks(v))
    s = jnp.einsum('brnqhd,brnkhd->brnhqk', qb, kk) * (d ** -0.5)
    qi = jnp.arange(ATT_BLOCK)[:, None]
    kj = jnp.arange(2 * ATT_BLOCK)[None, :]
    dist = qi + ATT_BLOCK - kj
    band = (dist >= 0) & (dist <= w_sub)
    has_prev = (jnp.arange(nb) > 0)[:, None, None] | (kj >= ATT_BLOCK)[None]
    mask = band[None] & has_prev
    s = jnp.where(mask[None, None, :, None], s, -jnp.inf)
    m = jnp.max(s, axis=-1, keepdims=True)
    p = jnp.exp(s - m)
    den = jnp.sum(p, axis=-1, keepdims=True)
    o = jnp.einsum('brnhqk,brnkhd->brnqhd', p / den, vv)
    lse = (m + jnp.log(den))[..., 0].transpose(0, 1, 2, 4, 3)
    o = o.reshape(b, r, Lp, h, d)[:, :, :L].transpose(0, 2, 1, 3, 4).reshape(b, S, h, d)
    lse = lse.reshape(b, r, Lp, h)[:, :, :L].transpose(0, 2, 1, 3).reshape(b, S, h)
    return o, lse

def dilated_attention_branch(q, k, v):
    outs, lses = [], []
    for gi, (window, dilation) in enumerate(ATT_PATTERNS):
        sl = slice(gi * ATT_HEADS_PER_GROUP, (gi + 1) * ATT_HEADS_PER_GROUP)
        o, lse = dilated_window_group(q[:, :, sl], k[:, :, sl], v[:, :, sl], window, dilation)
        outs.append(o)
        lses.append(lse)
    o = jnp.stack(outs, axis=0)
    wts = jax.nn.softmax(jnp.stack(lses, axis=0), axis=0)
    return jnp.sum(wts[..., None] * o, axis=0)

def second_inputs(seed: int = 0) -> dict:
    key = jax.random.key(seed)
    ks = jax.random.split(key, 20)
    f32 = jnp.float32

    def nrm(k, shape, scale):
        return jax.random.normal(k, shape, f32) * scale

    dt0 = jnp.exp(jax.random.uniform(ks[6], (DEPTH_2, SSM_N_HEADS), f32,
                                     minval=math.log(1e-3), maxval=math.log(1e-1)))
    return {
        "x": nrm(ks[0], (BATCH, SEQ, D_MODEL), 1.0),
        "norm_mix": 1.0 + nrm(ks[1], (DEPTH_2, D_MODEL), 0.05),
        "w_in": nrm(ks[2], (DEPTH_2, D_MODEL, IN_PROJ_DIM), D_MODEL ** -0.5),
        "b_gate": nrm(ks[3], (DEPTH_2, N_BRANCH * D_MODEL), 0.01),
        "conv_w": nrm(ks[4], (DEPTH_2, SSM_CONV, SSM_CONV_DIM), SSM_CONV ** -0.5),
        "conv_b": nrm(ks[5], (DEPTH_2, SSM_CONV_DIM), 0.01),
        "dt_bias": dt0 + jnp.log(-jnp.expm1(-dt0)),
        "a_log": jnp.log(jax.random.uniform(ks[7], (DEPTH_2, SSM_N_HEADS), f32, minval=1.0, maxval=16.0)),
        "d_skip": 1.0 + nrm(ks[8], (DEPTH_2, SSM_N_HEADS), 0.1),
        "ssm_norm": 1.0 + nrm(ks[9], (DEPTH_2, SSM_D_INNER), 0.05),
        "w_ssm_out": nrm(ks[10], (DEPTH_2, SSM_D_INNER, D_MODEL), SSM_D_INNER ** -0.5),
        "w_att_out": nrm(ks[11], (DEPTH_2, ATT_OUT_DIM, D_MODEL), ATT_OUT_DIM ** -0.5),
        "w_mix_out": nrm(ks[12], (DEPTH_2, D_MODEL, D_MODEL), D_MODEL ** -0.5),
        "norm_ffn": 1.0 + nrm(ks[13], (DEPTH_2, D_MODEL), 0.05),
        "w_ffn_gate": nrm(ks[14], (DEPTH_2, D_MODEL, D_FF_2), D_MODEL ** -0.5),
        "w_ffn_up": nrm(ks[15], (DEPTH_2, D_MODEL, D_FF_2), D_MODEL ** -0.5),
        "w_ffn_down": nrm(ks[16], (DEPTH_2, D_FF_2, D_MODEL), D_FF_2 ** -0.5),
        "norm_final": 1.0 + nrm(ks[17], (D_MODEL,), 0.05),
    }

def second_block(x, norm_mix, w_in, b_gate, conv_w, conv_b, dt_bias, a_log, d_skip, ssm_norm,
              w_ssm_out, w_att_out, w_mix_out, norm_ffn, w_ffn_gate, w_ffn_up, w_ffn_down, norm_final):
    b, S, _ = x.shape
    pos = jnp.arange(S)
    offs = [0]
    for sz in IN_PROJ_SIZES[:-1]:
        offs.append(offs[-1] + sz)
    for l in range(DEPTH_2):
        h = rmsnorm_2(x, norm_mix[l])
        proj = h @ w_in[l]
        z, xBC, dt_raw, qkv, gate_logits = jnp.split(proj, offs[1:], axis=-1)

        y_ssm = mamba2_branch(z, xBC, dt_raw, conv_w[l], conv_b[l], dt_bias[l], a_log[l],
                              d_skip[l], ssm_norm[l]) @ w_ssm_out[l]

        qkv = qkv.astype(jnp.float32).reshape(b, S, 3, ATT_N_HEADS, ATT_HEAD_DIM)
        q = rope(qkv[:, :, 0], pos)
        k = rope(qkv[:, :, 1], pos)
        v = qkv[:, :, 2]
        y_att = dilated_attention_branch(q, k, v).reshape(b, S, ATT_OUT_DIM).astype(x.dtype) @ w_att_out[l]

        gates = jax.nn.sigmoid((gate_logits + b_gate[l]).astype(jnp.float32))
        gates = gates.reshape(b, S, N_BRANCH, D_MODEL).astype(x.dtype)
        mixed = gates[:, :, 0] * y_ssm + gates[:, :, 1] * y_att
        x = x + mixed @ w_mix_out[l]

        h = rmsnorm_2(x, norm_ffn[l])
        x = x + (jax.nn.silu(h @ w_ffn_gate[l]) * (h @ w_ffn_up[l])) @ w_ffn_down[l]
    return rmsnorm_2(x, norm_final)


def setup_inputs(seed=0):
    out = dict(first_inputs(seed))
    for name, value in second_inputs(seed + 1).items():
        if name != "x":
            out[name + "_2"] = value
    return out


def reference(
    x, positions, ffn1_norm, ffn1_w_gate, ffn1_w_up, ffn1_w_down, mix_norm, w_in, mla_q_norm,
    mla_w_qb, mla_kv_norm, mla_w_kvb, conv_dw_w, conv_dw_b, conv_ln_g, conv_ln_b, hy_short_w,
    hy_short_b, hy_filt_w1, hy_filt_b1, hy_filt_w2, hy_filt_b2, hy_filt_w3, hy_filt_b3,
    hy_filt_w4, hy_filt_freq, hy_bias_d, out_norm, w_out, ffn2_norm, ffn2_w_gate, ffn2_w_up,
    ffn2_w_down, final_norm, norm_mix_2, w_in_2, b_gate_2, conv_w_2, conv_b_2, dt_bias_2,
    a_log_2, d_skip_2, ssm_norm_2, w_ssm_out_2, w_att_out_2, w_mix_out_2, norm_ffn_2,
    w_ffn_gate_2, w_ffn_up_2, w_ffn_down_2, norm_final_2,
):
    x = first_block(
        x, positions, ffn1_norm, ffn1_w_gate, ffn1_w_up, ffn1_w_down, mix_norm, w_in,
        mla_q_norm, mla_w_qb, mla_kv_norm, mla_w_kvb, conv_dw_w, conv_dw_b, conv_ln_g,
        conv_ln_b, hy_short_w, hy_short_b, hy_filt_w1, hy_filt_b1, hy_filt_w2, hy_filt_b2,
        hy_filt_w3, hy_filt_b3, hy_filt_w4, hy_filt_freq, hy_bias_d, out_norm, w_out, ffn2_norm,
        ffn2_w_gate, ffn2_w_up, ffn2_w_down, final_norm,
    )
    return second_block(
        x, norm_mix_2, w_in_2, b_gate_2, conv_w_2, conv_b_2, dt_bias_2, a_log_2, d_skip_2,
        ssm_norm_2, w_ssm_out_2, w_att_out_2, w_mix_out_2, norm_ffn_2, w_ffn_gate_2, w_ffn_up_2,
        w_ffn_down_2, norm_final_2,
    )


_drawn_inputs = setup_inputs


def setup_inputs(seed=0):
    import zlib

    import numpy as np

    out = dict(_drawn_inputs(seed))
    spreads = {}
    factors = {'conv_ln_b': 3.616, 'hy_filt_freq': 5.08, 'b_gate_2': 26.432, 'conv_b_2': 8.0}
    for name, (base, spread) in spreads.items():
        noise = np.random.default_rng([zlib.crc32(name.encode()), seed]).standard_normal(out[name].shape)
        drawn = base * np.exp(spread * noise) if base else spread * noise
        out[name] = __import__('jax').numpy.asarray(drawn.astype(out[name].dtype))
    for name, factor in factors.items():
        out[name] = (out[name] * factor).astype(out[name].dtype)
    return out
```

```python
from contextlib import ExitStack, contextmanager

import concourse.bass as bass
from concourse import mybir
from concourse.alu_op_type import AluOpType as ALU

import numpy as np

ACT = mybir.ActivationFunctionType
F32 = mybir.dt.float32
F32R = mybir.dt.float32r
AX_X = mybir.AxisListType.X

P = 128
T = 512
D = 1024
DC = D // P
F = 2816
FC = F // P
LAYERS = 2
EPS = 1e-6
BLOCK = 8
RAW = 4
FFN_BLOCKS = 2 * FC + 2 * (FC // 2)
IN_BLOCKS = 14
LAYER_BLOCKS = 2 * FFN_BLOCKS + IN_BLOCKS + 4 + 8

HEADS, NOPE, ROPE, V_DIM = 8, 64, 32, 64
QK = NOPE + ROPE
TAPS, SHORT = 31, 3
CW = 256
CT = CW // P
FILT, EMB = 64, 33
TT = T // P
FT = T // P
TWO_PI = 2.0 * np.pi
PI_A = 6.28125
PI_B = 0.0019350051879882812
PI_C = float(TWO_PI - PI_A - PI_B)
ROUND = 12582912.0
PI_MAX = 3.1415925
(Q_NORM, KV_NORM, CONV_W, CONV_B, LN_G, LN_B, SHORT_W, SHORT_B, FILT_B, FILT_FREQ, BIAS_D, OUT_NORM,
 LAYER_COLS) = np.cumsum([0, 2, 1, CT * TAPS, CT, CT, CT, 3 * CT * SHORT, 3 * CT, 3, 1, 2 * CT, 8]).tolist()


HD, GROUPS = 128, 3
RES = 4
SG, SH, CH = 4, 8, T // P
SSM_TILES = 6
SSM_ORDER = (4, 5, 0, 1, 2, 3)
SSM_TAPS = 4
MASKED = -1e30
G_CONV_W, G_CONV_B, G_SKIP, G_NORM, GROUP_COLS = np.cumsum([0, SSM_TILES * SSM_TAPS, SSM_TILES, 4, 4]).tolist()

DT_COLS = SG * GROUP_COLS + 16

SLOT_STEPS = {
    "pe": {"w_split": 10, "tile_free": 9, "vt_ready": 3, "v_timed": 3, "soft_ready": 4, "soft_copied": 4,
           "soft_tail": 4, "soft_shifted": 4, "att_split": 1, "acc_free": 8, "qk_ready": 6},
    "act": {"v_turned": 3, "soft_shifted": 4, "soft_turned": 8, "att_mixed": 1},
    "dve": {"acc_free": 8, "tile_free": 9, "dve_step": 16, "tile_ready": 9, "soft_in": 4,
           "soft_shifted": 4, "soft_exp": 4, "soft_ready": 4, "att_rounded": 1, "att_split": 1,
           "acc_ready": 8, "qk_ready": 6},
}
GROUP_STEPS = {
    "pe": {"w_split": 14, "tile_free": 10, "norm_summed": 1, "norm_split": 4, "norm_rms": 1, "acc_free": 8,
           "group_dt": 1, "conv_out": 6, "x_timed": 4, "b_timed": 1, "rows_copied": 1, "x_decayed": 3,
           "cb_masked": 1, "state_done": 1, "reach_done": 8, "pair_decay": 4, "y_taken": 4},
    "act": {"norm_scaled": 4, "norm_sum": 1, "z_scaled": 4, "conv_in": 6, "rows_ready": 1, "gap_ready": 1,
           "b_turned": 1, "spread_ready": 4, "reach_in": 8, "y_taken": 4, "y_gated": 4},
    "dve": {"acc_free": 8, "tile_free": 10, "dve_step": 34, "tile_ready": 10, "norm_rms": 1,
           "norm_scaled": 4, "norm_squared": 4, "norm_rounded": 4, "norm_split": 4, "acc_ready": 8,
           "z_out": 4, "group_dt": 1, "conv_in": 6, "sums_ready": 1, "gap_ready": 1, "left_ready": 2,
           "x_turned": 4, "x_timed": 4, "x_decayed": 3, "cb_ready": 1, "cb_masked": 1, "state_in": 3,
           "state_done": 1, "spread_ready": 4, "reach_in": 8, "reach_exp": 8, "reach_done": 8,
           "y_parts": 4, "y_taken": 4, "y_gated": 4},
}
LAYER_STEPS = {
    "pe": {"pair_free": 44, "w_split": 158, "x_split": 24, "x_summed": 24, "hidden_split": 44,
           "tile_free": 14, "ln_in": 1, "ln_squared": 2, "layer_loaded": 96, "filt_sine": 3,
           "spec_free": 24, "taps_magnitude": 8, "even_ready": 8, "signal_ready": 2, "signal_timed": 4,
           "out_spec_ready": 8, "norm_summed": 5, "norm_split": 11, "norm_rms": 6, "q_copied": 8,
           "q_roped": 8, "k_copied": 4, "v_copied": 4, "probs_ready": 32, "probs_scaled": 32,
           "turned_copied": 32, "mixed_copied": 8, "dft_loaded0": 16, "dft_loaded1": 16, "dft_loaded2": 16,
           "dft_loaded3": 16},
    "act": {"x_summed": 24, "sum_ready": 3, "gate_scaled": 44, "hidden_ready": 44, "x_updated": 24,
           "layer_loaded": 96, "gate_in": 2, "ln_centered": 2, "ln_sum": 2, "norm_scaled": 10,
           "filt_angle": 3, "taps_decayed": 8, "taps_summed": 8, "spec_ready": 8, "signal_turned": 4,
           "norm_in": 5, "norm_sum": 5, "q_ready": 8, "k_ready": 4, "v_ready": 4, "shift_ready": 32,
           "turned_ready": 32, "latent_ready": 1},
    "dve": {"pair_free": 44, "tile_free": 14, "x_rounded": 24, "x_split": 24, "x_squared": 24,
           "dve_step": 177, "x_summed": 24, "rms_ready": 3, "gate_ready": 44, "gate_scaled": 44,
           "up_ready": 44, "gate_activated": 44, "hidden_ready": 44, "hidden_rounded": 44,
           "hidden_split": 44, "out_ready": 24, "x_updated": 24, "layer_loaded": 96, "tile_ready": 14,
           "gate_out": 2, "ln_sum": 2, "ln_centered": 2, "norm_rms": 6, "norm_scaled": 10, "ln_out": 2,
           "filt_sum": 3, "filt_angle": 3, "taps_ready": 8, "taps_decayed": 8, "even_ready": 8,
           "taps_summed": 8, "spec_ready": 8, "taps_magnitude": 8, "freq_ready": 8, "out_spec_ready": 8,
           "convolved": 4, "norm_squared": 11, "norm_rounded": 11, "norm_split": 11, "q_ready": 8,
           "q_roped": 8, "scores_ready": 32, "shift_ready": 32, "probs_ready": 32, "probs_scaled": 32,
           "mixed_ready": 8, "mixed_copied": 8, "long_done": 1},
}


class Engine:

    def __init__(self, engine, passed):
        self.engine, self.passed = engine, passed
        self.sem_inc, self.dma_start, self.Fori = engine.sem_inc, engine.dma_start, engine.Fori

    def wait_ge(self, sem, value):
        self.engine.wait_ge(sem, value)
        if not isinstance(value, int):
            self.engine.sem_inc(self.passed, 1)


class Counts:

    def __init__(self, engine):
        self.engine, self.value = engine, {}

    def at(self, sem):
        base, off = self.value.get(sem.name, (0, 0))
        return base + off

    def add(self, sem, k=1):
        base, off = self.value.get(sem.name, (0, 0))
        self.value[sem.name] = (base, off + k)
        return k

    def next(self, sem, k=1):
        self.add(sem, k)
        return self.at(sem)

    @contextmanager
    def loop(self, times, steps):
        before = dict(self.value)
        with self.engine.Fori(0, times) as i:
            for name, k in steps.items():
                base, off = before.get(name, (0, 0))
                self.value[name] = (i * k + base + off, 0)
            start = dict(self.value)
            yield i
        moved = {n: self.value[n][1] - start.get(n, (0, 0))[1] for n in self.value}
        moved = {n: k for n, k in moved.items() if k}
        assert moved == steps, f"a pass moves {moved}, said {steps}"
        for name, k in steps.items():
            base, off = before.get(name, (0, 0))
            self.value[name] = (base, off + k * times)


def build(nc, io):
    ctx = ExitStack()
    with ctx:
        def sb(name, shape, dt=F32, where=ctx):
            return where.enter_context(nc.sbuf_tensor(name, shape, dt))

        def sem(name):
            return ctx.enter_context(nc.semaphore(name))

        NB = io["w"].shape[0]
        bank = [ctx.enter_context(nc.psum_tensor(f"bank{i}", [P, 512], F32)) for i in range(8)]
        RING = (5, 6, 7, 0, 1, 2, 3)
        SUM_BANK = 4
        VALUE_BANKS = (3, SUM_BANK, 5)
        Z_BANKS = (5, 6, 7, SUM_BANK)
        raw = sb("raw", [P, RAW, BLOCK * P])
        w_hi = sb("w_hi", [P, 2, BLOCK * P], F32R)
        w_lo = sb("w_lo", [P, 2, BLOCK * P], F32R)
        x = sb("x", [P, DC, T])
        x_hi = sb("x_hi", [P, DC, T], F32R)
        x_lo = sb("x_lo", [P, DC, T], F32R)
        square = sb("square", [P, 4, T])
        square_sum = sb("square_sum", [P, T])
        rstd = sb("rstd", [P, T])
        ones = sb("ones", [P, P])
        eps = sb("eps", [P, 1])
        gains = sb("gains", [P, 10 * DC])
        ident = sb("ident", [P, P])
        layer_cols = sb("layer_cols", [P, LAYER_COLS])
        rope_cols = sb("rope_cols", [P, 2])
        trig = sb("trig", [P, T])
        start_mem = ExitStack()
        positions = sb("positions", [P, T], mybir.dt.int32, start_mem)
        trig_tmp = sb("trig_tmp", [P, T], F32, start_mem)
        start_mem.close()
        ffn_mem = ExitStack()
        hidden_hi = sb("hidden_hi", [P, FC, T], F32R, ffn_mem)
        hidden_lo = sb("hidden_lo", [P, FC, T], F32R, ffn_mem)
        gate = sb("gate", [P, T], F32, ffn_mem)
        gate_silu = sb("gate_silu", [P, T], F32, ffn_mem)
        up = sb("up", [P, T], F32, ffn_mem)
        hidden = sb("hidden", [P, T], F32, ffn_mem)
        ffn_mem.close()

        mix_mem = ExitStack()
        y = sb("y", [P, DC, T], F32, mix_mem)
        latent = sb("latent", [P, 3, T], F32, mix_mem)
        key_rope = sb("key_rope", [P, T], F32, mix_mem)
        scaled = sb("scaled", [P, 2, T], F32, mix_mem)
        mix_rms = sb("mix_rms", [P, T], F32, mix_mem)
        hyena_mem = ExitStack()
        short = sb("short", [P, 3 * CT, T], F32, hyena_mem)
        dft = sb("dft", [P, 2, TT, T], F32, hyena_mem)
        spectrum = sb("spectrum", [P, FT, 2, 2, CW], F32, hyena_mem)
        decay = sb("decay", [P, TT, CW], F32, hyena_mem)
        decay_back = sb("decay_back", [P, 1], F32, hyena_mem)
        long_pad = sb("long_pad", [P, CT, T + TAPS - 1], F32, hyena_mem)
        filt_w = sb("filt_w", [FILT, 3 * FILT + 4 * CW], F32, hyena_mem)
        filt_z = sb("filt_z", [EMB, T], F32, hyena_mem)
        conv_mem = ExitStack()
        short_pad = sb("short_pad", [P, 3 * CT, T + SHORT - 1], F32, conv_mem)
        conv_mem.close()
        filt_mem = ExitStack()
        taps = sb("taps", [P, 2, 2, CW], F32, filt_mem)
        taps_abs = sb("taps_abs", [P, 2, 2, CW], F32, filt_mem)
        tap_norm = sb("tap_norm", [P, CW], F32, filt_mem)
        v_time = sb("v_time", [P, TT, CW], F32, filt_mem)
        even_mem = ExitStack()
        even_odd = sb("even_odd", [P, 2, TT, CW], F32, even_mem)
        even_mem.close()
        out_spectrum = sb("out_spectrum", [P, 2, FT, CW], F32, filt_mem)
        filt_mem.close()
        hyena_mem.close()
        tap_products = (rstd[:], square[:, 3, :])
        conv_acc = y[:, 0:CT, :]
        angle, turns, filt_h = (square[0:FILT, i, :] for i in range(3))
        products = square[:, 0:2, :].rearrange("p a (b n) -> p (a b) n", b=2)
        conv_a, conv_g, conv_s = (square[:, i, :] for i in range(3))
        y_split = [sb(f"y_{part}", [P, DC - CT, T], F32R, mix_mem) for part in ("hi", "lo")]
        y_hi, y_lo = ([xs[:, 4 + i, :] for i in range(CT)] + [ys[:, i, :] for i in range(DC - CT)]
                      for xs, ys in zip((x_hi, x_lo), y_split))
        latent_hi, latent_lo = ([xs[:, k, :] for k in (6, 7, 3)] for xs in (x_hi, x_lo))
        mla_k = sb("mla_k", [P, 4, T], F32, mix_mem)
        mla_q = sb("mla_q", [P, 4, T], F32, mix_mem)
        mla_v = sb("mla_v", [P, TT, 4 * V_DIM], F32, mix_mem)
        probs = sb("probs", [P, 2, TT, T], F32, mix_mem)
        rope_c, rope_d = square[:, 2, :], square[:, 3, :]
        rope_a, rope_b, probs_t = square[:, 0, :], square[:, 1, :], square[:, 2:4, :]
        row_max = sb("row_max", [P, TT], F32, mix_mem)
        row_shift = sb("row_shift", [P, TT], F32, mix_mem)
        row_sum = sb("row_sum", [P, TT], F32, mix_mem)
        row_inv = sb("row_inv", [P, TT], F32, mix_mem)
        mix_mem.close()
        two_mem = ExitStack()
        att_sum = sb("att_sum", [P, DC, T], F32, two_mem)
        ssm_sum = sb("ssm_sum", [P, DC, T], F32, two_mem)
        cols2 = sb("cols2", [P, SG * GROUP_COLS + 16 + 2], F32, two_mem)
        dt_time = sb("dt_time", [P, 2, CH, SG * SH], F32, two_mem)
        tri = sb("tri", [P, P], F32, two_mem)
        att_mem = ExitStack()
        dt_rows = sb("dt_rows", [SG * SH, 5, T], F32, att_mem)
        a_exp = sb("a_exp", [SG * SH, 1], F32, att_mem)
        mask = sb("mask", [P, RES, T + 2 * P], F32, att_mem)
        turn2 = sb("turn2", [P, 2, T], F32, att_mem)
        rot = sb("rot", [P, 2, T], F32, att_mem)
        att_qk = sb("att_qk", [P, 2 * GROUPS, T], F32, att_mem)
        att_vt = sb("att_vt", [P, GROUPS, T], F32, att_mem)
        att_v = sb("att_v", [P, GROUPS, T], F32, att_mem)
        soft = sb("soft", [P, 2, T + 2 * P], F32, att_mem)
        soft_t = sb("soft_t", [P, 2, T + 2 * P], F32, att_mem)
        soft_max = sb("soft_max", [P, 2], F32, att_mem)
        soft_shift = sb("soft_shift", [P, 2], F32, att_mem)
        soft_sum = sb("soft_sum", [P, 2], F32, att_mem)
        att_hi = sb("att_hi", [P, T], F32R, att_mem)
        att_lo = sb("att_lo", [P, T], F32R, att_mem)
        att_mem.close()
        ssm_mem = ExitStack()
        sel = sb("sel", [SH, 12 * P], F32, ssm_mem)
        gcols = sb("gcols", [P, GROUP_COLS], F32, ssm_mem)
        dt_g = sb("dt_g", [P, 2, CH, SH], F32, ssm_mem)
        a_cum = sb("a_cum", [P, 2, CH, SH], F32, ssm_mem)
        a_gap = sb("a_gap", [P, CH, SH], F32, ssm_mem)
        a_own = sb("a_own", [P, CH, SH], F32, ssm_mem)
        a_left = sb("a_left", [P, CH, SH], F32, ssm_mem)
        a_whole = sb("a_whole", [P, CH, SH], F32, ssm_mem)
        a_rows = sb("a_rows", [SH, T], F32, ssm_mem)
        xbc = sb("xbc", [P, SSM_TILES, T], F32, ssm_mem)
        z_act = sb("z_act", [P, 4, T], F32, ssm_mem)
        z_in = sb("z_in", [P, T], F32, ssm_mem)
        cb = sb("cb", [P, T], F32, ssm_mem)
        state = sb("state", [P, CH - 1, T], F32, ssm_mem)
        reach = sb("reach", [P, 4, T], F32, ssm_mem)
        x_time = sb("x_time", [P, CH, T], F32, ssm_mem)
        two_in_mem = ExitStack()
        xbc_pad = sb("xbc_pad", [P, SSM_TILES, T + SSM_TAPS - 1], F32, two_in_mem)
        x_left = sb("x_left", [P, CH - 1, T], F32, two_in_mem)
        b_time = sb("b_time", [P, CH, P], F32, two_in_mem)
        two_in_mem.close()
        scaled2 = sb("scaled2", [P, 2, T], F32, ssm_mem)
        rms2 = sb("rms2", [P, T], F32, ssm_mem)
        ssm_hi = sb("ssm_hi", [P, 4, T], F32R, ssm_mem)
        ssm_lo = sb("ssm_lo", [P, 4, T], F32R, ssm_mem)
        ssm_mem.close()
        gate_a = sb("gate_a", [P, 2, T], F32, two_mem)
        gate_b = sb("gate_b", [P, 2, T], F32, two_mem)
        merged = sb("merged", [P, T], F32, two_mem)
        merged_hi = sb("merged_hi", [P, DC, T], F32R, two_mem)
        merged_lo = sb("merged_lo", [P, DC, T], F32R, two_mem)
        two_mem.close()

        w_loaded = [sem(f"w_loaded{i}") for i in range(RAW)]
        w_rounded, w_split, w_begun = sem("w_rounded"), sem("w_split"), sem("w_begun")
        pool_passed, pe_passed, act_passed, dve_passed = (
            sem(n) for n in ("pool_passed", "pe_passed", "act_passed", "dve_passed"))
        consts_loaded, gains_loaded = sem("consts_loaded"), sem("gains_loaded")
        x_loaded, x_rest_loaded = sem("x_loaded"), sem("x_rest_loaded")
        consts_set = sem("consts_set")
        dve_step, act_step = sem("dve_step"), sem("act_step")
        x_updated, x_rounded, x_squared, x_summed, x_split = (
            sem("x_updated"), sem("x_rounded"), sem("x_squared"), sem("x_summed"), sem("x_split"))
        sum_ready, rms_ready = sem("sum_ready"), sem("rms_ready")
        gate_ready, up_ready = sem("gate_ready"), sem("up_ready")
        pair_free = sem("pair_free")
        gate_scaled, gate_activated = sem("gate_scaled"), sem("gate_activated")
        hidden_ready, hidden_rounded, hidden_split = (
            sem("hidden_ready"), sem("hidden_rounded"), sem("hidden_split"))
        out_ready = sem("out_ready")
        y_ready = sem("y_ready")
        stored = sem("stored")
        two_loaded, group_loaded = sem("two_loaded"), sem("group_loaded")
        dt_raw, dt_magnitude, dt_log, dt_done, dt_turned = (
            sem(n) for n in ("dt_raw", "dt_magnitude", "dt_log", "dt_done", "dt_turned"))
        dt_timed = sem("dt_timed")
        qk_ready, vt_ready, v_turned, v_timed = (
            sem(n) for n in ("qk_ready", "vt_ready", "v_turned", "v_timed"))
        soft_in, soft_shifted, soft_exp, soft_ready, soft_turned, soft_copied, soft_tail = (
            sem(n) for n in ("soft_in", "soft_shifted", "soft_exp", "soft_ready", "soft_turned",
                             "soft_copied", "soft_tail"))
        att_mixed, att_rounded, att_split = (
            sem(n) for n in ("att_mixed", "att_rounded", "att_split"))
        acc_ready, acc_free = sem("acc_ready"), sem("acc_free")
        conv_in, conv_out, z_scaled, z_out, group_dt = (
            sem(n) for n in ("conv_in", "conv_out", "z_scaled", "z_out", "group_dt"))
        sums_ready, rows_ready, rows_copied, gap_ready, left_ready = (
            sem(n) for n in ("sums_ready", "rows_ready", "rows_copied", "gap_ready", "left_ready"))
        x_turned, x_timed, b_turned, b_timed, cb_ready, cb_masked, x_decayed, state_in, state_done = (
            sem(n) for n in ("x_turned", "x_timed", "b_turned", "b_timed", "cb_ready", "cb_masked",
                             "x_decayed", "state_in", "state_done"))
        spread_ready, reach_in, reach_exp, reach_done, pair_decay, y_parts, y_taken = (
            sem(n) for n in ("spread_ready", "reach_in", "reach_exp", "reach_done", "pair_decay",
                             "y_parts", "y_taken"))
        y_gated = sem("y_gated")
        gate_logit, gate_open, merged_ready, merged_rounded, merged_split = (
            sem(n) for n in ("gate_logit", "gate_open", "merged_ready", "merged_rounded", "merged_split"))
        trig_angle, trig_sine = sem("trig_angle"), sem("trig_sine")
        layer_loaded, dft_loaded = sem("layer_loaded"), [sem(f"dft_loaded{f}") for f in range(FT)]
        tile_ready, tile_free = sem("tile_ready"), sem("tile_free")
        latent_ready = sem("latent_ready")
        gate_in, gate_out = sem("gate_in"), sem("gate_out")
        long_tap, long_done = sem("long_tap"), sem("long_done")
        norm_in, norm_squared, norm_summed, norm_sum, norm_rms, norm_scaled, norm_rounded, norm_split = (
            sem(n) for n in ("norm_in", "norm_squared", "norm_summed", "norm_sum", "norm_rms",
                             "norm_scaled", "norm_rounded", "norm_split"))
        ln_in, ln_centered, ln_squared, ln_sum, ln_out = (
            sem(n) for n in ("ln_in", "ln_centered", "ln_squared", "ln_sum", "ln_out"))
        filt_sum, filt_angle, filt_sine = sem("filt_sum"), sem("filt_angle"), sem("filt_sine")
        taps_ready, taps_decayed, taps_magnitude, taps_summed = (
            sem("taps_ready"), sem("taps_decayed"), sem("taps_magnitude"), sem("taps_summed"))
        even_ready, spec_ready, spec_free = sem("even_ready"), sem("spec_ready"), sem("spec_free")
        signal_ready, signal_turned, signal_timed = (
            sem("signal_ready"), sem("signal_turned"), sem("signal_timed"))
        freq_ready, out_spec_ready, convolved = sem("freq_ready"), sem("out_spec_ready"), sem("convolved")
        q_ready, q_copied, k_ready, k_copied, v_ready, v_copied, q_roped = (
            sem(n) for n in ("q_ready", "q_copied", "k_ready", "k_copied", "v_ready", "v_copied", "q_roped"))
        scores_ready, shift_ready, probs_ready, probs_scaled = (
            sem(n) for n in ("scores_ready", "shift_ready", "probs_ready", "probs_scaled"))
        turned_ready, turned_copied, mixed_ready, mixed_copied = (
            sem(n) for n in ("turned_ready", "turned_copied", "mixed_ready", "mixed_copied"))

        block = ctx.enter_context(nc.Block())

        @block.sync
        def _(sp):
            sp.dma_start(gains[:], io["gains"]).then_inc(gains_loaded, 16)
            sp.dma_start(x[:, 0:4, :], io["x"][:, 0:4]).then_inc(x_loaded, 16)
            sp.dma_start(raw[:, 0, :], io["w"][0]).then_inc(w_loaded[0], 16)
            sp.dma_start(x[:, 4:8, :], io["x"][:, 4:8]).then_inc(x_rest_loaded, 16)
            for s in range(1, RAW):
                sp.dma_start(raw[:, s, :], io["w"][s]).then_inc(w_loaded[s], 16)
            for to, name in ((ident, "ident"), (rope_cols, "rope_cols"), (positions, "positions")):
                sp.dma_start(to[:], io[name]).then_inc(consts_loaded, 16)
            with sp.Fori(1, NB // RAW) as i:
                for s in range(RAW):
                    sp.wait_ge(w_split, i * RAW + (s + 1 - RAW))
                    sp.dma_start(raw[:, s, :], io["w"][bass.ds(i * RAW + s, 1)].rearrange("a p n -> p (a n)")
                                 ).then_inc(w_loaded[s], 16)
            for n in range(DC // 2):
                sp.wait_ge(y_ready, 2 * n + 2)
                sp.dma_start(io["out"][:, 2 * n:2 * n + 2], x[:, 2 * n:2 * n + 2, :]).then_inc(stored, 16)
            sp.wait_ge(stored, 16 * (DC // 2))

        @block.gpsimd
        def _(pool):
            nc.gpsimd.memset(ones[:], 1.0).then_inc(consts_set, 1)
            nc.gpsimd.memset(eps[:], EPS).then_inc(consts_set, 1)

            def split_block(n, i, s, reuse):
                pool.wait_ge(w_loaded[s], i * 16 + 16)
                pool.sem_inc(pool_passed, 1)
                if reuse:
                    pool.wait_ge(w_begun, n)
                    pool.sem_inc(pool_passed, 1)
                nc.gpsimd.tensor_scalar(w_hi[:, s % 2, :], raw[:, s, :], 1.0, 0.0, ALU.mult, ALU.add
                                        ).then_inc(w_rounded, 1)
                pool.wait_ge(w_rounded, n + 1)
                nc.gpsimd.tensor_tensor(w_lo[:, s % 2, :], raw[:, s, :], w_hi[:, s % 2, :].bitcast(F32),
                                        ALU.subtract).then_inc(w_split, 1)

            def split_blocks(first, end):
                passes = (end - first) // RAW
                if passes:
                    with pool.Fori(0, passes) as i:
                        for k in range(first, first + RAW):
                            split_block(i * RAW + k, i + k // RAW, k % RAW, True)
                for n in range(first + passes * RAW, end):
                    split_block(n, n // RAW, n % RAW, True)

            def long_conv(l):
                acc, ended = conv_acc[:, 0, :], l * (2 * TAPS - 1)

                def issue(ins):
                    nonlocal ended
                    ins.then_inc(long_tap, 1)
                    ended += 1
                    return ended

                def tap(j):
                    return issue(nc.gpsimd.tensor_scalar(tap_products[j % 2], long_pad[:, 0, j:j + T],
                                                         layer_cols[:, CONV_W + j:CONV_W + j + 1], 0.0,
                                                         ALU.mult, ALU.add))

                pool.wait_ge(latent_ready, l + 1)
                added = issue(nc.gpsimd.tensor_scalar(acc, long_pad[:, 0, 0:T], layer_cols[:, CONV_W:CONV_W + 1],
                                                      layer_cols[:, CONV_B:CONV_B + 1], ALU.mult, ALU.add))
                product = tap(1)
                for j in range(1, TAPS):
                    pool.wait_ge(long_tap, added)
                    this = product
                    if j + 1 < TAPS:
                        product = tap(j + 1)
                    pool.wait_ge(long_tap, max(this, added))
                    added = issue(nc.gpsimd.tensor_tensor(acc, acc, tap_products[j % 2], ALU.add))
                pool.wait_ge(long_tap, added)
                pool.sem_inc(long_done, 1)

            for n in range(RAW):
                split_block(n, 0, n, n >= 2)
            at = RAW
            for l in range(LAYERS):
                end = l * LAYER_BLOCKS + FFN_BLOCKS + IN_BLOCKS + 1
                split_blocks(at, end)
                long_conv(l)
                at = end
            split_blocks(at, NB)

        @block.tensor
        def _(pe):
            pe = Engine(pe, pe_passed)
            c = Counts(pe)
            slot = [0]
            fresh = [False]
            pe.wait_ge(consts_set, 2)

            def take():
                pe.wait_ge(w_split, c.next(w_split))
                s = slot[0]
                slot[0] ^= 1
                fresh[0] = True
                return s

            def product(out, s, t, hi, lo, start, stop):
                hi_w, lo_w = w_hi[:, s, t * P:(t + 1) * P], w_lo[:, s, t * P:(t + 1) * P]
                first = nc.tensor.matmul(out, hi_w, hi, start=start, stop=False)
                if fresh[0]:
                    first.then_inc(w_begun, 1)
                    fresh[0] = False
                nc.tensor.matmul(out, hi_w, lo, start=False, stop=False)
                return nc.tensor.matmul(out, lo_w, hi, start=False, stop=stop)

            def project(out, arriving=0):
                s = take()
                for k in range(DC):
                    if arriving and (k == 0 or k >= arriving):
                        pe.wait_ge(x_split, c.next(x_split, 1 if k else arriving))
                    last = product(out, s, k, x_hi[:, k, :], x_lo[:, k, :], k == 0, k == DC - 1)
                return last

            def sum_squares():
                pe.wait_ge(x_summed, c.next(x_summed, DC))
                nc.tensor.matmul(bank[SUM_BANK][:], ones[:], square_sum[:], start=True, stop=True
                                 ).then_inc(sum_ready, 1)

            def down(hi, lo, pairs, wait_inputs):
                for half in range(2):
                    banks = bank[4:8] if half == 0 else bank[0:4]

                    def pair(j, start, stop):
                        s = take()
                        if half == 0 and wait_inputs is not None:
                            pe.wait_ge(wait_inputs, c.next(wait_inputs, 2))
                        for a in range(2):
                            k = 2 * j + a
                            at = (lambda v: v[k] if isinstance(v, list) else v[:, k, :]) if isinstance(k, int) else (
                                lambda v: v[:, bass.ds(k, 1), :].rearrange("p a n -> p (a n)"))
                            for m in range(4):
                                last = product(banks[m][:], s, 4 * a + m, at(hi), at(lo),
                                               start and a == 0, stop and a == 1)
                                if stop and a == 1:
                                    last.then_inc(out_ready, 1)

                    pair(0, True, False)
                    if pairs > 4:
                        steps = {"w_split": 2}
                        if half == 0 and wait_inputs is not None:
                            steps[wait_inputs.name] = 4
                        with c.loop((pairs - 3) // 2, steps) as i:
                            pair(2 * i + 1, False, False)
                            pair(2 * i + 2, False, False)
                        pair(pairs - 2, False, False)
                    else:
                        pair(1, False, False)
                        pair(2, False, False)
                    pair(pairs - 1, False, True)

            def ffn():
                def two_tiles(first=False):
                    for b in range(2):
                        pe.wait_ge(pair_free, c.next(pair_free))
                        project(bank[2 * b][:], arriving=5 if first and b == 0 else 0).then_inc(gate_ready, 1)
                        project(bank[2 * b + 1][:]).then_inc(up_ready, 1)
                        if first and b == 0:
                            sum_squares()

                two_tiles(first=True)
                with c.loop(FC // 2 - 1, {"pair_free": 2, "w_split": 4}):
                    two_tiles()
                down(hidden_hi, hidden_lo, FC // 2, hidden_split)

            def norm_sum_matmul(n, to=SUM_BANK):
                pe.wait_ge(norm_summed, c.next(norm_summed))
                nc.tensor.matmul(bank[to][:], ones[:], (square_sum[:] if n > 1 else square[:, 0, :]),
                                 start=True, stop=True).then_inc(norm_sum, 1)

            def in_projection(tiles, between):
                for n in range(tiles):
                    pe.wait_ge(tile_free, c.next(tile_free))
                    project(bank[RING[n % len(RING)]][:], arriving=2 if n == 0 else 0).then_inc(tile_ready, 1)
                    if n in between:
                        between[n]()

            def layer_norm_sum(what):
                if what == 0:
                    pe.wait_ge(ln_in, c.next(ln_in))
                else:
                    pe.wait_ge(ln_squared, c.next(ln_squared, CT))
                for i in range(CT):
                    src = conv_acc[:, i, :] if what == 0 else square[:, 2 + i, :]
                    last = nc.tensor.matmul(bank[SUM_BANK][:], ones[:], src, start=i == 0, stop=i == CT - 1)
                last.then_inc(ln_sum, 1)

            def filter_layer(i):
                if i:
                    pe.wait_ge(filt_sine, c.next(filt_sine))
                else:
                    pe.wait_ge(layer_loaded, c.next(layer_loaded, 16 * 6))
                    pe.wait_ge(norm_rms, c.next(norm_rms))
                k, rhs = ((EMB, filt_z), (FILT, filt_h), (FILT, filt_h))[i]
                nc.tensor.matmul(bank[SUM_BANK][0:FILT, :], filt_w[0:k, i * FILT:(i + 1) * FILT], rhs[0:k, :],
                                 start=True, stop=True).then_inc(filt_sum, 1)

            def hyena_filters():
                pe.wait_ge(filt_sine, c.next(filt_sine))
                pe.wait_ge(tile_free, c.at(tile_free) + len(RING))
                for o in range(2):
                    def taps_of(t):
                        pe.wait_ge(spec_free, c.next(spec_free))
                        w4 = 3 * FILT + o * 2 * CW
                        nc.tensor.matmul(bank[t % 2][:], filt_h[:, t * P:(t + 1) * P],
                                         filt_w[:, w4:w4 + 2 * CW], start=True, stop=True
                                         ).then_inc(taps_ready, 1)

                    taps_of(0)
                    for t in range(TT):
                        if t + 1 < TT:
                            taps_of(t + 1)
                        pe.wait_ge(taps_magnitude, c.next(taps_magnitude))
                        for way in range(2):
                            last = nc.tensor.matmul(bank[6][:, 0:CW], ones[:], taps_abs[:, t % 2, way, :],
                                                    start=t == 0 and way == 0, stop=t == TT - 1 and way == 1)
                        last.then_inc(taps_summed, 1)
                    pe.wait_ge(even_ready, c.next(even_ready, TT))
                    for f in range(FT):
                        pe.wait_ge(spec_free, c.next(spec_free))
                        for part in range(2):
                            for t in range(TT):
                                last = nc.tensor.matmul(bank[f % 2][:, part * CW:(part + 1) * CW],
                                                        dft[:, part, t, f * P:(f + 1) * P],
                                                        even_odd[:, part, t, :], start=t == 0, stop=t == TT - 1)
                        last.then_inc(spec_ready, 1)

            def long_convolution(o):
                pe.wait_ge(signal_ready, c.next(signal_ready))
                for t in range(TT):
                    for i in range(CT):
                        at = (t % 2) * CW + i * P
                        src = short if o == 0 else y
                        tile = i if o == 0 else 2 + i
                        last = nc.tensor.transpose(bank[2 + t // 2][:, at:at + P],
                                                   src[:, tile, t * P:(t + 1) * P], ident[:])
                    if t % 2:
                        last.then_inc(signal_turned, 1)
                pe.wait_ge(signal_timed, c.next(signal_timed, 2))
                for f in range(FT):
                    pe.wait_ge(spec_free, c.next(spec_free))
                    if o == 0:
                        pe.wait_ge(dft_loaded[f], c.next(dft_loaded[f], 16))
                    for part in range(2):
                        for t in range(TT):
                            last = nc.tensor.matmul(bank[f % 2][:, part * CW:(part + 1) * CW],
                                                    dft[:, part, t, f * P:(f + 1) * P], v_time[:, t, :],
                                                    start=t == 0, stop=t == TT - 1)
                    last.then_inc(freq_ready, 1)
                for i in range(CT):
                    for f in range(FT):
                        if o == 0 and i == 1 and f == FT - 1:
                            layer_norm_sum(1)
                        if i == 0:
                            pe.wait_ge(out_spec_ready, c.next(out_spec_ready))
                            if o == 0 and f == FT - 1:
                                layer_norm_sum(0)
                            elif f == FT - 1:
                                norm_sum_matmul(2)
                        for part in range(2):
                            last = nc.tensor.matmul(bank[2 + i][:], out_spectrum[:, part, f, i * P:(i + 1) * P],
                                                    dft[:, part, f, :], start=f == 0 and part == 0,
                                                    stop=f == FT - 1 and part == 1)
                    last.then_inc(convolved, 1)

            def mla():
                norm_sum_matmul(2)
                pe.wait_ge(norm_split, c.next(norm_split, 3))
                pe.wait_ge(norm_rms, c.next(norm_rms, 3))
                with c.loop(2, {"w_split": 2, "q_copied": 4, "q_roped": 4, "k_copied": 2, "v_copied": 2,
                                "probs_ready": 16, "probs_scaled": 16, "turned_copied": 16,
                                "mixed_copied": 4}):
                    s = take()
                    for h in range(4):
                        for k in range(2):
                            last = product(bank[h][:], s, 2 * h + k, latent_hi[k], latent_lo[k],
                                           k == 0, k == 1)
                        last.then_inc(q_ready, 1)
                    s = take()
                    for pair in range(2):
                        product(bank[5 + pair][:], s, pair, latent_hi[2], latent_lo[2],
                                True, True).then_inc(k_ready, 1)
                    cols = slice(2 * P, 4 * P)
                    for t in range(TT):
                        out = bank[7 if t < 2 else SUM_BANK][:, (t % 2) * 2 * P:(t % 2 + 1) * 2 * P]
                        hi, lo = (v[2][:, t * P:(t + 1) * P] for v in (latent_hi, latent_lo))
                        nc.tensor.matmul(out, hi, w_hi[:, s, cols], start=True, stop=False)
                        nc.tensor.matmul(out, hi, w_lo[:, s, cols], start=False, stop=False)
                        last = nc.tensor.matmul(out, lo, w_hi[:, s, cols], start=False, stop=True)
                        if t % 2:
                            last.then_inc(v_ready, 1)
                    pe.wait_ge(k_copied, c.next(k_copied, 2))

                    def scores(h):
                        for t in range(TT):
                            if h:
                                pe.wait_ge(probs_ready, c.next(probs_ready))
                            else:
                                pe.wait_ge(q_copied, c.next(q_copied))
                                pe.wait_ge(q_roped, c.next(q_roped))
                            nc.tensor.matmul(bank[t][:], mla_q[0:QK, h, t * P:(t + 1) * P], mla_k[0:QK, h, :],
                                             start=True, stop=True).then_inc(scores_ready, 1)

                    scores(0)
                    pe.wait_ge(v_copied, c.next(v_copied, 2))
                    for h in range(4):
                        if h < 3:
                            scores(h + 1)
                        else:
                            c.add(probs_ready, TT)
                        pe.wait_ge(probs_scaled, c.next(probs_scaled, TT))

                        def turn(kt):
                            for t in range(TT):
                                last = nc.tensor.transpose(bank[5 + kt % 2][:, t * P:(t + 1) * P],
                                                           probs[:, h % 2, t, kt * P:(kt + 1) * P], ident[:])
                            last.then_inc(turned_ready, 1)

                        turn(0)
                        for kt in range(TT):
                            if kt + 1 < TT:
                                turn(kt + 1)
                            pe.wait_ge(turned_copied, c.next(turned_copied))
                            if h and kt == 0:
                                pe.wait_ge(mixed_copied, c.next(mixed_copied))
                            last = nc.tensor.matmul(bank[7][0:V_DIM, :], mla_v[:, kt, h * V_DIM:(h + 1) * V_DIM],
                                                    probs_t[:, kt % 2, :], start=kt == 0, stop=kt == TT - 1)
                        last.then_inc(mixed_ready, 1)
                    pe.wait_ge(mixed_copied, c.next(mixed_copied))
                norm_sum_matmul(4, to=0)
                c.add(norm_rms)

            def mixer():
                def latent_norm(n):
                    if n == 2:
                        pe.wait_ge(norm_rms, c.next(norm_rms))
                    norm_sum_matmul(n)

                in_projection(IN_BLOCKS, {1: sum_squares, 4: lambda: latent_norm(1), 6: lambda: latent_norm(2),
                                   8: lambda: filter_layer(0), 10: lambda: filter_layer(1),
                                   12: lambda: filter_layer(2)})
                hyena_filters()
                long_convolution(0)
                long_convolution(1)
                mla()
                down(y_hi, y_lo, 4, norm_split)

            with c.loop(LAYERS, LAYER_STEPS["pe"]):
                ffn()
                mixer()
                ffn()

            def accumulate(hi, lo, tiles):
                per = BLOCK // tiles
                for m in range(DC):
                    if m % per == 0:
                        s = take()
                    pe.wait_ge(acc_free, c.next(acc_free))
                    for k in range(tiles):
                        last = product(bank[m % 4][:], s, (m % per) * tiles + k, hi[k], lo[k],
                                       k == 0, k == tiles - 1)
                    last.then_inc(acc_ready, 1)

            def ring_tiles(n_tiles):
                for n in range(n_tiles):
                    if n == 3:
                        pe.wait_ge(acc_free, c.at(acc_free) + 4)
                    pe.wait_ge(tile_free, c.next(tile_free))
                    project(bank[RING[n % len(RING)]][:]).then_inc(tile_ready, 1)

            def value_tile(b):
                pe.wait_ge(tile_free, c.next(tile_free))
                pe.wait_ge(tile_free, c.at(tile_free) + len(RING) - 1)
                project(bank[b][:]).then_inc(tile_ready, 1)

            def attention_slot(more):
                pe.wait_ge(tile_free, c.at(tile_free) + len(RING))
                ring_tiles(2 * GROUPS)
                pe.wait_ge(vt_ready, c.next(vt_ready, GROUPS))
                for g in range(GROUPS):
                    if VALUE_BANKS[g] == RING[0]:
                        pe.wait_ge(tile_free, c.at(tile_free) + len(RING) + 1 - 2 * GROUPS)
                    for t in range(RES):
                        last = nc.tensor.transpose(bank[VALUE_BANKS[g]][:, t * P:(t + 1) * P],
                                                   att_vt[:, g, t * P:(t + 1) * P], ident[:])
                    last.then_inc(v_turned, 1)
                pe.wait_ge(v_timed, c.next(v_timed, GROUPS))
                pe.wait_ge(qk_ready, c.next(qk_ready, 2 * GROUPS))

                def scores(r):
                    if r >= 2:
                        pe.wait_ge(soft_shifted, c.next(soft_shifted))
                    rows = slice(r * P, (r + 1) * P)
                    nc.tensor.matmul(bank[r % 2][:], att_qk[:, 0, rows], att_qk[:, GROUPS, :],
                                     start=True, stop=True)
                    for g in (1, 2):
                        last = nc.tensor.matmul(bank[2 + r % 2][:, (g - 1) * P:g * P], att_qk[:, g, rows],
                                                att_qk[:, GROUPS + g, rows], start=True, stop=True)
                    last.then_inc(soft_in, 1)

                scores(0)
                for r in range(RES):
                    if r + 1 < RES:
                        scores(r + 1)
                    pe.wait_ge(soft_ready, c.next(soft_ready))
                    for n in range(RES + 2):
                        to = bank[5][:, n * P:(n + 1) * P] if n < RES else bank[6][:, (n - RES) * P:(n - RES + 1) * P]
                        last = nc.tensor.transpose(to, soft[:, r % 2, n * P:(n + 1) * P], ident[:])
                        if n == RES - 1 or n == RES + 1:
                            last.then_inc(soft_turned, 1)
                    if more and r < GROUPS:
                        value_tile(SUM_BANK)
                    pe.wait_ge(soft_copied, c.next(soft_copied))
                    pe.wait_ge(soft_tail, c.next(soft_tail))
                    for n in range(RES + 2):
                        g, key = (0, n) if n < RES else (n - RES + 1, r)
                        last = nc.tensor.matmul(bank[7][:, r * P:(r + 1) * P], att_v[:, g, key * P:(key + 1) * P],
                                                soft_t[:, r % 2, n * P:(n + 1) * P], start=n == 0, stop=n == RES + 1)
                last.then_inc(att_mixed, 1)
                c.add(soft_shifted, 2)
                pe.wait_ge(att_split, c.next(att_split))
                accumulate([att_hi[:]], [att_lo[:]], 1)

            def z_tiles(after_norm):
                for i, b in enumerate(Z_BANKS):
                    pe.wait_ge(tile_free, c.next(tile_free))
                    if after_norm and b == SUM_BANK:
                        pe.wait_ge(norm_rms, c.next(norm_rms))
                    project(bank[b][:]).then_inc(tile_ready, 1)

            def ssm_group(more):
                pe.wait_ge(tile_free, c.at(tile_free) + len(RING))
                ring_tiles(SSM_TILES)
                pe.wait_ge(tile_free, c.at(tile_free) + len(RING))
                pe.wait_ge(group_dt, c.next(group_dt))
                a_g = dt_g[:, 1].rearrange("p c h -> p (c h)")
                nc.tensor.matmul(bank[5][:, 0:CH * SH], tri[:], a_g, start=True, stop=True)
                nc.tensor.matmul(bank[5][:, CH * SH:2 * CH * SH], ones[:], a_g, start=True, stop=True
                                 ).then_inc(sums_ready, 1)
                for ch in range(CH):
                    last = nc.tensor.matmul(bank[6][0:SH, ch * P:(ch + 1) * P], dt_g[:, 1, ch, :], tri[:],
                                            start=True, stop=True)
                last.then_inc(rows_ready, 1)
                pe.wait_ge(conv_out, c.next(conv_out, 2))
                for ch in range(CH):
                    last = nc.tensor.transpose(bank[2][:, ch * P:(ch + 1) * P],
                                               xbc[:, 4, ch * P:(ch + 1) * P], ident[:])
                last.then_inc(b_turned, 1)
                for ch in range(CH):
                    rows = slice(ch * P, (ch + 1) * P)
                    last = nc.tensor.matmul(bank[3][:, rows], xbc[:, 4, rows], xbc[:, 5, rows],
                                            start=True, stop=True)
                last.then_inc(cb_ready, 1)
                pe.wait_ge(conv_out, c.next(conv_out, 4))
                for ch in range(CH):
                    if ch >= 2:
                        pe.wait_ge(x_timed, c.next(x_timed))
                    for i in range(4):
                        last = nc.tensor.transpose(bank[ch % 2][:, i * P:(i + 1) * P],
                                                   xbc[:, i, ch * P:(ch + 1) * P], ident[:])
                    last.then_inc(x_turned, 1)
                pe.wait_ge(b_timed, c.next(b_timed))
                pe.wait_ge(rows_copied, c.next(rows_copied))
                for ch in range(CH - 1):
                    pe.wait_ge(x_decayed, c.next(x_decayed))
                    nc.tensor.matmul(bank[5 + ch][:], b_time[:, ch, :], x_left[:, ch, :], start=True, stop=True
                                     ).then_inc(state_in, 1)
                pe.wait_ge(x_timed, c.next(x_timed, 2))
                pe.wait_ge(cb_masked, c.next(cb_masked))

                def spread(pair):
                    banks = ((0, 1, 2), (6, 7, SUM_BANK))[pair % 2]
                    for n, b in zip((2 * pair, 2 * pair + 1, SH + pair), banks):
                        last = nc.tensor.matmul(bank[b][:], sel[:, n * P:(n + 1) * P], a_rows[:],
                                                start=True, stop=True)
                    last.then_inc(spread_ready, 1)

                spread(0)
                pe.wait_ge(state_done, c.next(state_done))
                for pair in range(4):
                    if pair + 1 < 4:
                        spread(pair + 1)
                    pe.wait_ge(reach_done, c.next(reach_done, 2))
                    pe.wait_ge(pair_decay, c.next(pair_decay))
                    if pair:
                        pe.wait_ge(y_taken, c.next(y_taken))
                    for b in range(2):
                        h = 2 * pair + b
                        for ch in range(CH):
                            nc.tensor.matmul(bank[3][b * 64:(b + 1) * 64, ch * P:(ch + 1) * P],
                                             x_time[:, ch, h * 64:(h + 1) * 64],
                                             reach[:, 2 * (pair % 2) + b, ch * P:(ch + 1) * P],
                                             start=True, stop=True)
                    for ch in range(1, CH):
                        last = nc.tensor.matmul(bank[5][:, ch * P:(ch + 1) * P],
                                                state[:, ch - 1, pair * P:(pair + 1) * P],
                                                xbc[:, 5, ch * P:(ch + 1) * P], start=True, stop=True)
                    last.then_inc(y_parts, 1)
                pe.wait_ge(y_taken, c.next(y_taken))
                norm_sum_matmul(4)
                if more:
                    z_tiles(True)
                else:
                    for n, b in enumerate(Z_BANKS):
                        if b == SUM_BANK:
                            pe.wait_ge(norm_rms, c.next(norm_rms))
                        project(bank[b][:]).then_inc((gate_ready, up_ready)[n % 2], 1)
                pe.wait_ge(norm_split, c.next(norm_split, 4))
                accumulate([ssm_hi[:, k, :] for k in range(4)], [ssm_lo[:, k, :] for k in range(4)], 4)

            def second_mixer():
                pe.wait_ge(tile_free, c.next(tile_free))
                project(bank[RING[-1]][:], arriving=1).then_inc(tile_ready, 1)
                sum_squares()
                for b in RING[:GROUPS]:
                    pe.wait_ge(tile_free, c.next(tile_free))
                    project(bank[b][:]).then_inc(tile_ready, 1)
                with c.loop(3, SLOT_STEPS["pe"]):
                    attention_slot(True)
                attention_slot(False)
                pe.wait_ge(acc_free, c.at(acc_free) + 4)
                pe.wait_ge(dt_done, c.next(dt_done, 2))
                for what in range(2):
                    for t in range(CH):
                        at = (what * CH + t) * SG * SH
                        last = nc.tensor.transpose(bank[0][:, at:at + SG * SH],
                                                   dt_rows[:, what, t * P:(t + 1) * P],
                                                   ident[0:SG * SH, 0:SG * SH])
                last.then_inc(dt_turned, 1)
                pe.wait_ge(dt_timed, c.next(dt_timed))
                z_tiles(False)
                with c.loop(SG - 1, GROUP_STEPS["pe"]):
                    ssm_group(True)
                ssm_group(False)
                pe.wait_ge(acc_free, c.at(acc_free) + 4)
                with c.loop(DC // 2 - 1, {"pair_free": 2, "w_split": 4}):
                    for b in range(2):
                        pe.wait_ge(pair_free, c.next(pair_free))
                        project(bank[2 * b][:]).then_inc(gate_ready, 1)
                        project(bank[2 * b + 1][:]).then_inc(up_ready, 1)
                down(merged_hi, merged_lo, 4, merged_split)

            c.add(x_split, DC)
            sum_squares()
            second_mixer()
            ffn()
            c.add(x_split, DC)
            sum_squares()

        @block.scalar
        def _(act):
            act = Engine(act, act_passed)
            c = Counts(act)
            act.wait_ge(consts_set, 2)

            def prepare(m, stage, wait):
                act.wait_ge(wait, c.next(wait) if wait is x_updated else 16)
                at = stage * DC + m
                g = gains[:, at:at + 1] if isinstance(at, int) else gains[:, bass.ds(at, 1)]
                nc.scalar.activation(x_hi[:, m, :], x[:, m, :], ACT.Copy, scale=g).then_inc(x_rounded, 1)
                if m >= 4:
                    act.wait_ge(x_summed, c.next(x_summed))
                nc.scalar.activation(square[:, m % 4, :], x[:, m, :], ACT.Square).then_inc(x_squared, 1)
                if m == DC - 1:
                    c.add(x_summed, 4)

            def rms():
                act.wait_ge(sum_ready, c.next(sum_ready))
                nc.scalar.activation(rstd[:], bank[SUM_BANK][:], ACT.Sqrt, bias=eps[:], scale=1.0 / D
                                     ).then_inc(rms_ready, 1)

            def ffn(stage):
                rms()
                with c.loop(FC, {"gate_scaled": 1, "hidden_ready": 1}) as f:
                    act.wait_ge(gate_scaled, c.next(gate_scaled))
                    nc.scalar.activation(gate_silu[:], gate[:], ACT.Silu).then_inc(gate_activated, 1)
                    act.wait_ge(hidden_ready, c.next(hidden_ready))
                    nc.scalar.activation(hidden_hi[:, bass.ds(f, 1), :].rearrange("p a n -> p (a n)"),
                                         hidden[:], ACT.Copy).then_inc(hidden_rounded, 1)
                for m in range(DC):
                    prepare(m, stage + 1, x_updated)

            def link(ins, done=act_step):
                ins.then_inc(done, c.add(done))
                act.wait_ge(done, c.at(done))

            def norm(srcs, hi_lo, width, at=SUM_BANK, out=mix_rms, via=scaled, sq=0):
                act.wait_ge(norm_in, c.next(norm_in))
                for i, src in enumerate(srcs):
                    nc.scalar.activation(square[:, sq + i, :], src, ACT.Square).then_inc(norm_squared, 1)
                norm_rest(hi_lo, width, at, out, via)

            def norm_rest(hi_lo, width, at=SUM_BANK, out=mix_rms, via=scaled):
                act.wait_ge(norm_sum, c.next(norm_sum))
                nc.scalar.activation(out[:], bank[at][:], ACT.Sqrt, bias=eps[:], scale=1.0 / width
                                     ).then_inc(norm_rms, 1)
                for i, hi in enumerate(hi_lo):
                    act.wait_ge(norm_scaled, c.next(norm_scaled))
                    nc.scalar.activation(hi, via[:, i % 2, :], ACT.Copy).then_inc(norm_rounded, 1)

            def load_layer(l):
                act.dma_start(decay_back[:], io["decay_back"]).then_inc(layer_loaded, 16)
                act.dma_start(layer_cols[:], io["layer_cols"][bass.ds(l, 1)].rearrange("a p n -> p (a n)")
                              ).then_inc(layer_loaded, 16)
                act.dma_start(filt_w[:], io["filt_w"][bass.ds(l, 1)].rearrange("a p n -> p (a n)")
                              ).then_inc(layer_loaded, 16)
                act.dma_start(filt_z[:], io["filt_z"]).then_inc(layer_loaded, 16)
                act.dma_start(decay[:], io["decay"]).then_inc(layer_loaded, 16)
                act.dma_start(dft[:], io["dft"][0]).then_inc(layer_loaded, 16)
                act.wait_ge(layer_loaded, c.next(layer_loaded, 16 * 6))

            def mixer(l, stage):
                load_layer(l)
                rms()
                def conv_gate():
                    act.wait_ge(gate_in, c.next(gate_in))
                    nc.scalar.activation(conv_s, conv_g, ACT.Sigmoid).then_inc(gate_out, 1)

                norm([latent[:, 2, :]], [], P)
                conv_gate()
                norm([latent[:, i, :] for i in (0, 1)], [], 2 * P)
                conv_gate()
                for i in range(3):
                    act.wait_ge(filt_angle, c.next(filt_angle))
                    nc.scalar.activation(filt_h, angle, ACT.Sin).then_inc(filt_sine, 1)
                act.wait_ge(latent_ready, c.next(latent_ready))
                for i in (2, 0, 1):
                    nc.scalar.activation(latent_hi[i], latent[:, i, :], ACT.Copy).then_inc(norm_rounded, 1)
                for n in range(2 * TT):
                    act.wait_ge(taps_decayed, c.next(taps_decayed))
                    if n >= 2:
                        act.wait_ge(taps_summed, c.at(taps_summed) + n - 1)
                    nc.scalar.activation(taps_abs[:, n % 2], taps[:, n % 2], ACT.Abs).then_inc(taps_magnitude, 1)
                c.add(taps_summed, 2 * TT)
                c.add(spec_ready, FT)
                for f in range(FT):
                    act.wait_ge(spec_ready, c.next(spec_ready))
                    cols = slice(f * P, (f + 1) * P)
                    act.dma_start(dft[:, :, :, cols], io["dft"][1][:, :, :, cols]).then_inc(dft_loaded[f], 16)
                for o in range(2):
                    for t in range(2):
                        act.wait_ge(signal_turned, c.next(signal_turned))
                        nc.scalar.activation(v_time[:, 2 * t:2 * t + 2, :].rearrange("p t n -> p (t n)"),
                                             bank[2 + t][:], ACT.Copy).then_inc(signal_timed, 1)
                    if o == 0:
                        for i in range(CT):
                            act.wait_ge(ln_centered, c.next(ln_centered))
                            nc.scalar.activation(square[:, 2 + i, :], conv_acc[:, i, :], ACT.Square
                                                 ).then_inc(ln_squared, 1)
                        act.wait_ge(ln_sum, c.next(ln_sum, 2))
                        nc.scalar.activation(mix_rms[:], bank[SUM_BANK][:], ACT.Sqrt, bias=eps[:],
                                             scale=1.0 / CW).then_inc(norm_rms, 1)
                    else:
                        for i in range(CT):
                            act.wait_ge(norm_scaled, c.next(norm_scaled))
                            nc.scalar.activation(y[:, i, :], scaled[:, i, :], ACT.Silu,
                                                 bias=layer_cols[:, LN_B + i:LN_B + i + 1]).then_inc(ln_out, 1)
                        norm([y[:, i, :] for i in (0, 1)], y_hi[0:2], CW, sq=2)
                mla(stage)

            def mla(stage):
                norm([y[:, i, :] for i in (2, 3)], y_hi[2:4], CW)
                with c.loop(2, {"q_ready": 4, "k_ready": 2, "v_ready": 2, "shift_ready": 16,
                                "turned_ready": 16}):
                    for h in range(4):
                        act.wait_ge(q_ready, c.next(q_ready))
                        nc.scalar.activation(mla_q[0:NOPE, h, :], bank[h][0:NOPE, :], ACT.Copy
                                             ).then_inc(q_copied, 1)
                    for pair in range(2):
                        act.wait_ge(k_ready, c.next(k_ready))
                        for b in range(2):
                            last = nc.scalar.activation(mla_k[0:NOPE, 2 * pair + b, :],
                                                        bank[5 + pair][b * NOPE:(b + 1) * NOPE, :], ACT.Copy)
                        last.then_inc(k_copied, 1)
                    for t in range(2):
                        act.wait_ge(v_ready, c.next(v_ready))
                        nc.scalar.activation(mla_v[:, 2 * t:2 * t + 2, :].rearrange("p t n -> p (t n)"),
                                             bank[7 if t == 0 else SUM_BANK][:], ACT.Copy
                                             ).then_inc(v_copied, 1)
                    def exponential(h, t):
                        act.wait_ge(shift_ready, c.next(shift_ready))
                        nc.scalar.activation(probs[:, h % 2, t, :], bank[t][:], ACT.Exp,
                                             bias=row_shift[:, t:t + 1], scale=QK ** -0.5,
                                             accum_out=row_sum[:, t:t + 1]).then_inc(probs_ready, 1)

                    for t in range(TT):
                        exponential(0, t)
                    for h in range(4):
                        for kt in range(TT):
                            act.wait_ge(turned_ready, c.next(turned_ready))
                            nc.scalar.activation(probs_t[:, kt % 2, :], bank[5 + kt % 2][:], ACT.Copy
                                                 ).then_inc(turned_copied, 1)
                            if h < 3:
                                exponential(h + 1, kt)
                norm([y[:, 4 + i, :] for i in range(4)], y_hi[4:8], T, at=0)
                for m in range(DC):
                    prepare(m, stage + 1, x_updated)

            def second_mixer():
                for to, name in ((cols2, "cols2"), (tri, "tri"), (mask, "mask"), (turn2, "turn2")):
                    act.dma_start(to[:], io[name]).then_inc(two_loaded, 16)
                rms()
                act.wait_ge(two_loaded, c.next(two_loaded, 64))
                heads = SG * SH
                act.wait_ge(dt_raw, c.next(dt_raw))
                link(nc.scalar.activation(dt_rows[:, 1, :], dt_rows[:, 0, :], ACT.Abs))
                link(nc.scalar.activation(dt_rows[:, 1, :], dt_rows[:, 1, :], ACT.Exp, scale=-1.0))
                nc.scalar.activation(a_exp[:], cols2[0:heads, DT_COLS + 1:DT_COLS + 2], ACT.Exp
                                     ).then_inc(dt_magnitude, 1)
                act.wait_ge(dt_log, c.next(dt_log))
                nc.scalar.activation(dt_rows[:, 3, :], dt_rows[:, 2, :], ACT.Ln).then_inc(dt_magnitude, 1)

                with c.loop(4, SLOT_STEPS["act"]):
                    for g in range(GROUPS):
                        act.wait_ge(v_turned, c.next(v_turned))
                        nc.scalar.activation(att_v[:, g, :], bank[VALUE_BANKS[g]][:], ACT.Copy).then_inc(v_timed, 1)

                    def exponentials(r):
                        act.wait_ge(soft_shifted, c.next(soft_shifted))
                        nc.scalar.activation(soft[:, r % 2, :], soft[:, r % 2, :], ACT.Exp,
                                             bias=soft_shift[:, r % 2:r % 2 + 1],
                                             accum_out=soft_sum[:, r % 2:r % 2 + 1]).then_inc(soft_exp, 1)

                    exponentials(0)
                    for r in range(RES):
                        act.wait_ge(soft_turned, c.next(soft_turned))
                        nc.scalar.activation(soft_t[:, r % 2, 0:T], bank[5][:], ACT.Copy).then_inc(soft_copied, 1)
                        act.wait_ge(soft_turned, c.next(soft_turned))
                        nc.scalar.activation(soft_t[:, r % 2, T:T + 2 * P], bank[6][:, 0:2 * P], ACT.Copy
                                             ).then_inc(soft_tail, 1)
                        if r + 1 < RES:
                            exponentials(r + 1)
                    act.wait_ge(att_mixed, c.next(att_mixed))
                    turned = bank[7][:].rearrange("p (r i) -> p i r", r=RES)
                    nc.scalar.activation(att_hi[:].rearrange("p (i r) -> p i r", r=RES), turned, ACT.Copy
                                         ).then_inc(att_rounded, 1)

                act.wait_ge(dt_turned, c.next(dt_turned))
                act.dma_start(sel[:], io["sel"]).then_inc(group_loaded, 16)
                nc.scalar.activation(dt_time[:].rearrange("p a c h -> p (a c h)"),
                                     bank[0][:, 0:2 * CH * SG * SH], ACT.Copy).then_inc(dt_timed, 1)
                act.wait_ge(group_loaded, c.next(group_loaded, 16))

                def z_silu():
                    for i in range(4):
                        act.wait_ge(z_scaled, c.next(z_scaled))
                        nc.scalar.activation(z_act[:, i, :], z_in[:], ACT.Silu).then_inc(z_out, 1)

                def square_of(pair):
                    act.wait_ge(y_gated, c.next(y_gated))
                    nc.scalar.activation(square[:, pair, :], xbc[:, pair, :], ACT.Square).then_inc(norm_squared, 1)

                def ssm_group(more):
                    for i in SSM_ORDER:
                        act.wait_ge(conv_in, c.next(conv_in))
                        nc.scalar.activation(xbc[:, i, :], xbc[:, i, :], ACT.Silu).then_inc(conv_out, 1)
                    act.wait_ge(rows_ready, c.next(rows_ready))
                    nc.scalar.activation(a_rows[:], bank[6][0:SH, :], ACT.Copy).then_inc(rows_copied, 1)
                    act.wait_ge(gap_ready, c.next(gap_ready))
                    nc.scalar.activation(a_left[:], a_gap[:], ACT.Exp).then_inc(left_ready, 1)
                    nc.scalar.activation(a_whole[:], a_cum[:, 1], ACT.Exp).then_inc(left_ready, 1)
                    act.wait_ge(b_turned, c.next(b_turned))
                    nc.scalar.activation(b_time[:].rearrange("p c n -> p (c n)"), bank[2][:], ACT.Copy
                                         ).then_inc(b_timed, 1)
                    for pair in range(4):
                        act.wait_ge(spread_ready, c.next(spread_ready))
                        if pair >= 2:
                            act.wait_ge(y_taken, c.next(y_taken))
                        nc.scalar.activation(scaled2[:, pair % 2, :], bank[(2, SUM_BANK)[pair % 2]][:], ACT.Exp
                                             ).then_inc(pair_decay, 1)
                        for b in range(2):
                            act.wait_ge(reach_in, c.next(reach_in))
                            at, h = 2 * (pair % 2) + b, 2 * pair + b
                            for ch in range(CH):
                                rows = slice(ch * P, (ch + 1) * P)
                                last = nc.scalar.activation(reach[:, at, rows], reach[:, at, rows], ACT.Exp,
                                                            bias=a_own[:, ch, h:h + 1])
                            last.then_inc(reach_exp, 1)
                        if pair:
                            square_of(pair - 1)
                    c.add(y_taken, 2)
                    square_of(3)
                    norm_rest([ssm_hi[:, i, :] for i in range(4)], T, out=rms2, via=scaled2)
                    if more:
                        z_silu()

                z_silu()
                with c.loop(SG - 1, GROUP_STEPS["act"]):
                    ssm_group(True)
                ssm_group(False)

                def merge(m):
                    for way in range(2):
                        act.wait_ge(gate_logit, c.next(gate_logit))
                        nc.scalar.activation(gate_b[:, way, :], gate_a[:, way, :], ACT.Sigmoid,
                                             bias=cols2[:, bass.ds(m + (SG * GROUP_COLS + 8 * way), 1)]
                                             ).then_inc(gate_open, 1)
                    act.wait_ge(merged_ready, c.next(merged_ready))
                    nc.scalar.activation(merged_hi[:, bass.ds(m, 1), :].rearrange("p a n -> p (a n)"),
                                         merged[:], ACT.Copy).then_inc(merged_rounded, 1)

                for m in range(2):
                    merge(m)
                with c.loop(DC // 2 - 1, {"gate_logit": 4, "merged_ready": 2}) as i:
                    for b in range(2):
                        merge(2 * i + (2 + b))
                for m in range(DC):
                    prepare(m, 7, x_updated)

            act.wait_ge(gains_loaded, 16)
            for m in range(DC):
                prepare(m, 0, x_loaded if m < 4 else x_rest_loaded)
            act.wait_ge(trig_angle, 1)
            nc.scalar.activation(trig[V_DIM:P, :], trig_tmp[V_DIM:P, :], ACT.Sin).then_inc(trig_sine, 1)
            with c.loop(LAYERS, LAYER_STEPS["act"]) as l:
                ffn(l * 3)
                mixer(l, l * 3 + 1)
                ffn(l * 3 + 2)
            rms()
            for m in range(DC):
                prepare(m, 6, x_updated)
            second_mixer()
            ffn(7)
            rms()

        @block.vector
        def _(dve):
            dve = Engine(dve, dve_passed)
            c = Counts(dve)
            dve.sem_inc(pair_free, 2)

            def link(ins, done=dve_step):
                ins.then_inc(done, c.add(done))
                dve.wait_ge(done, c.at(done))

            def rest(m, stage):
                dve.wait_ge(x_rounded, c.next(x_rounded))
                at = stage * DC + m
                g = gains[:, at:at + 1] if isinstance(at, int) else gains[:, bass.ds(at, 1)]
                link(nc.vector.scalar_tensor_tensor(x_lo[:, m, :], x[:, m, :], g, x_hi[:, m, :].bitcast(F32),
                                                    ALU.mult, ALU.subtract), x_split)

            def add_squares(chunks):
                for m in chunks:
                    dve.wait_ge(x_squared, c.next(x_squared))
                    if m == 1:
                        link(nc.vector.tensor_tensor(square_sum[:], square[:, 0, :], square[:, 1, :], ALU.add))
                        dve.sem_inc(x_summed, c.add(x_summed, 2))
                    elif m > 1:
                        link(nc.vector.tensor_tensor(square_sum[:], square_sum[:], square[:, m % 4, :], ALU.add),
                             x_summed)

            def absorb(stage, coef):
                for half in range(2):
                    banks = bank[4:8] if half == 0 else bank[0:4]
                    for b in range(4):
                        m = 4 * half + b
                        dve.wait_ge(out_ready, c.next(out_ready))
                        link(nc.vector.scalar_tensor_tensor(x[:, m, :], banks[b][:], coef, x[:, m, :],
                                                            ALU.mult, ALU.add), x_updated)
                        if b:
                            rest(m - 1, stage)
                    rest(m, stage)
                    add_squares(range(4 * half, 4 * half + 4))

            def reciprocal_rms():
                dve.wait_ge(rms_ready, c.next(rms_ready))
                link(nc.vector.reciprocal(rstd[:], rstd[:]))

            def ffn(stage, coef=0.5):
                reciprocal_rms()
                with c.loop(FC // 2, {"gate_ready": 2, "gate_scaled": 2, "up_ready": 2, "pair_free": 2,
                                      "gate_activated": 2, "hidden_ready": 2, "hidden_rounded": 2,
                                      "hidden_split": 2}) as i:
                    for b in range(2):
                        f = 2 * i + b
                        dve.wait_ge(gate_ready, c.next(gate_ready))
                        link(nc.vector.tensor_tensor(gate[:], bank[2 * b][:], rstd[:], ALU.mult), gate_scaled)
                        dve.wait_ge(up_ready, c.next(up_ready))
                        link(nc.vector.tensor_tensor(up[:], bank[2 * b + 1][:], rstd[:], ALU.mult), pair_free)
                        dve.wait_ge(gate_activated, c.next(gate_activated))
                        link(nc.vector.tensor_tensor(hidden[:], gate_silu[:], up[:], ALU.mult), hidden_ready)
                        dve.wait_ge(hidden_rounded, c.next(hidden_rounded))
                        at = lambda v: v[:, bass.ds(f, 1), :].rearrange("p a n -> p (a n)")
                        link(nc.vector.tensor_tensor(at(hidden_lo), hidden[:], at(hidden_hi).bitcast(F32),
                                                     ALU.subtract), hidden_split)
                absorb(stage + 1, coef)

            def reduce_angle(a, k):
                link(nc.vector.tensor_scalar(k, a, 1.0 / TWO_PI, ROUND, ALU.mult, ALU.add))
                link(nc.vector.tensor_scalar(k, k, ROUND, None, ALU.subtract))
                for part in (PI_A, PI_B, PI_C):
                    link(nc.vector.scalar_tensor_tensor(a, k, -part, a, ALU.mult, ALU.add))

            def norm_squares(n_tiles, sq=0):
                dve.sem_inc(norm_in, 1)
                for i in range(n_tiles):
                    dve.wait_ge(norm_squared, c.next(norm_squared))
                    if i == 1:
                        link(nc.vector.tensor_tensor(square_sum[:], square[:, sq, :], square[:, sq + 1, :],
                                                     ALU.add))
                    elif i > 1:
                        link(nc.vector.tensor_tensor(square_sum[:], square_sum[:], square[:, sq + i, :], ALU.add))
                dve.sem_inc(norm_summed, 1)

            def norm_scale(n_tiles, srcs, at, hi, lo, gain=layer_cols, out=mix_rms, via=scaled):
                dve.wait_ge(norm_rms, c.next(norm_rms))
                link(nc.vector.reciprocal(out[:], out[:]))

                def scale(i):
                    link(nc.vector.scalar_tensor_tensor(via[:, i % 2, :], srcs[i], gain[:, at + i:at + i + 1],
                                                        out[:], ALU.mult, ALU.mult), norm_scaled)

                scale(0)
                for i in range(n_tiles):
                    if i + 1 < n_tiles:
                        scale(i + 1)
                    dve.wait_ge(norm_rounded, c.next(norm_rounded))
                    link(nc.vector.tensor_tensor(lo[i], via[:, i % 2, :], hi[i].bitcast(F32), ALU.subtract),
                         norm_split)

            def norm(n_tiles, srcs, at, hi, lo, gain=layer_cols, out=mix_rms, via=scaled):
                norm_squares(n_tiles)
                norm_scale(n_tiles, srcs, at, hi, lo, gain, out, via)

            tile_no = [0]

            def tile_out(dst, rows=slice(0, P)):
                dve.wait_ge(tile_ready, c.next(tile_ready))
                b = bank[RING[tile_no[0] % len(RING)]]
                tile_no[0] += 1
                link(nc.vector.tensor_tensor(dst, b[rows, :], rstd[rows, :], ALU.mult), tile_free)

            def col(n, rows=P):
                return layer_cols[0:rows, n:n + 1]

            def mixer(stage):
                reciprocal_rms()
                tile_no[0] = 0
                dve.wait_ge(layer_loaded, c.next(layer_loaded, 16 * 6))
                link(nc.vector.memset(long_pad[:], 0.0))
                link(nc.vector.memset(short_pad[:], 0.0))

                def gated_input(i):
                    tile_out(conv_a)
                    tile_out(conv_g)
                    dve.sem_inc(gate_in, 1)
                    dve.wait_ge(gate_out, c.next(gate_out))
                    link(nc.vector.tensor_tensor(long_pad[:, i, TAPS // 2:TAPS // 2 + T], conv_a, conv_s,
                                                 ALU.mult))

                def depthwise(dst, src, n_taps, w, b):
                    link(nc.vector.tensor_scalar(dst, src(0), col(w), col(b), ALU.mult, ALU.add))
                    for j in range(1, n_taps):
                        link(nc.vector.scalar_tensor_tensor(dst, src(j), col(w + j), dst, ALU.mult, ALU.add))

                def short_tile(i):
                    tile_out(short_pad[:, i, 1:1 + T])
                    depthwise(short[:, i, :], lambda j: short_pad[:, i, j:j + T], SHORT, SHORT_W + i * SHORT,
                              SHORT_B + i)

                def long_tap_of_second(j):
                    acc, w, src = conv_acc[:, 1, :], col(CONV_W + TAPS + j), long_pad[:, 1, j:j + T]
                    if j == 0:
                        link(nc.vector.tensor_scalar(acc, src, w, col(CONV_B + 1), ALU.mult, ALU.add))
                    else:
                        link(nc.vector.scalar_tensor_tensor(acc, src, w, acc, ALU.mult, ALU.add))

                def filter_angle(i):
                    dve.wait_ge(filt_sum, c.next(filt_sum))
                    link(nc.vector.tensor_scalar(angle, bank[SUM_BANK][0:FILT, :], col(FILT_B + i, FILT),
                                                 col(FILT_FREQ, FILT), ALU.add, ALU.mult))
                    reduce_angle(angle, turns)
                    link(nc.vector.tensor_scalar(angle, angle, PI_MAX, -PI_MAX, ALU.min, ALU.max),
                         filt_angle)

                def latent_scale(tiles, at):
                    dve.wait_ge(norm_rms, c.next(norm_rms))
                    link(nc.vector.reciprocal(mix_rms[:], mix_rms[:]))
                    for n, i in enumerate(tiles):
                        link(nc.vector.scalar_tensor_tensor(latent[:, i, :], latent[:, i, :], col(at + n),
                                                            mix_rms[:], ALU.mult, ALU.mult))

                for i in (2, 0, 1):
                    tile_out(latent[:, i, :])
                norm_squares(1)
                dve.wait_ge(tile_ready, c.next(tile_ready))
                b = bank[RING[tile_no[0] % len(RING)]]
                tile_no[0] += 1
                link(nc.vector.tensor_tensor(rope_c[V_DIM:P, :], b[V_DIM:P, :], rstd[V_DIM:P, :], ALU.mult),
                     tile_free)
                link(nc.vector.tensor_tensor(rope_d[V_DIM:QK, :], rope_c[V_DIM:QK, :], trig[V_DIM:QK, :],
                                             ALU.mult))
                link(nc.vector.tensor_tensor(key_rope[V_DIM:QK, :], rope_c[QK:P, :], trig[QK:P, :], ALU.mult))
                link(nc.vector.tensor_tensor(key_rope[V_DIM:QK, :], key_rope[V_DIM:QK, :], rope_d[V_DIM:QK, :],
                                             ALU.add))
                latent_scale((2,), KV_NORM)
                gated_input(0)
                norm_squares(2)
                latent_scale((0, 1), Q_NORM)
                gated_input(1)
                for i in range(3):
                    filter_angle(i)
                    short_tile(2 * i)
                    short_tile(2 * i + 1)
                dve.sem_inc(latent_ready, 1)
                dve.sem_inc(signal_ready, 1)
                for o in range(2):
                    for t in range(TT):
                        dve.wait_ge(taps_ready, c.next(taps_ready))
                        if o or t >= 2:
                            dve.wait_ge(taps_magnitude, c.at(taps_magnitude) + o * TT + t - 1)
                        h = bank[t % 2][:].rearrange("p (a n) -> p a n", a=2)
                        both = decay[:, t:t + 1, :].broadcast_to([P, 2, CW])
                        link(nc.vector.tensor_tensor(taps[:, t % 2], h, both, ALU.mult),
                             taps_decayed if t else dve_step)
                        if t == 0:
                            link(nc.vector.tensor_scalar(taps[:, 0, 1, :], taps[:, 0, 1, :], decay_back[:],
                                                         None, ALU.mult), taps_decayed)
                        dve.sem_inc(spec_free, 1)
                        fwd, bwd = taps[:, t % 2, 0, :], taps[:, t % 2, 1, :]
                        nc.vector.tensor_tensor(even_odd[:, 0, t, :], fwd, bwd, ALU.add)
                        link(nc.vector.tensor_tensor(even_odd[:, 1, t, :], fwd, bwd, ALU.subtract), even_ready)
                    dve.wait_ge(taps_summed, c.next(taps_summed, TT))
                    link(nc.vector.reciprocal(tap_norm[:], bank[6][:, 0:CW]))
                    link(nc.vector.tensor_scalar(tap_norm[:], tap_norm[:], 1.0 / T, None, ALU.mult))
                    for f in range(FT):
                        first = 4 * (o * FT + f)
                        long_tap_of_second(first)
                        dve.wait_ge(spec_ready, c.next(spec_ready))
                        for part in range(2):
                            last = nc.vector.tensor_tensor(spectrum[:, f, o, part, :],
                                                           bank[f % 2][:, part * CW:(part + 1) * CW],
                                                           tap_norm[:], ALU.mult)
                        link(last)
                        dve.sem_inc(spec_free, 1)
                        for j in range(first + 1, min(first + 4, TAPS)):
                            long_tap_of_second(j)
                c.add(taps_magnitude, 2 * TT)

                for o in range(2):
                    if o == 0:
                        for i in (2, 0, 1):
                            dve.wait_ge(norm_rounded, c.next(norm_rounded))
                            link(nc.vector.tensor_tensor(latent_lo[i], latent[:, i, :], latent_hi[i].bitcast(F32),
                                                         ALU.subtract), norm_split)
                    else:
                        dve.sem_inc(signal_ready, 1)
                        dve.wait_ge(norm_rms, c.next(norm_rms))
                        link(nc.vector.reciprocal(mix_rms[:], mix_rms[:]))
                        for i in range(CT):
                            link(nc.vector.scalar_tensor_tensor(scaled[:, i, :], conv_acc[:, i, :], col(LN_G + i),
                                                                mix_rms[:], ALU.mult, ALU.mult), norm_scaled)
                        dve.wait_ge(ln_out, c.next(ln_out, 2))
                        norm_squares(2, sq=2)
                    for f in range(FT):
                        dve.wait_ge(freq_ready, c.next(freq_ready))
                        re, im = bank[f % 2][:, 0:CW], bank[f % 2][:, CW:2 * CW]
                        f_re, f_im = spectrum[:, f, o, 0, :], spectrum[:, f, o, 1, :]
                        for n, (a, b) in enumerate(((re, f_re), (im, f_im), (re, f_im), (im, f_re))):
                            last = nc.vector.tensor_tensor(products[:, n, :], a, b, ALU.mult)
                        link(last)
                        dve.sem_inc(spec_free, 1)
                        nc.vector.tensor_tensor(out_spectrum[:, 0, f, :], products[:, 0, :],
                                                products[:, 1, :], ALU.subtract)
                        link(nc.vector.tensor_tensor(out_spectrum[:, 1, f, :], products[:, 2, :],
                                                     products[:, 3, :], ALU.add), out_spec_ready)
                    if o == 0:
                        dve.wait_ge(long_done, c.next(long_done))
                        dve.sem_inc(ln_in, 1)
                        dve.wait_ge(ln_sum, c.next(ln_sum, 2) - 1)
                        for i in range(CT):
                            link(nc.vector.scalar_tensor_tensor(conv_acc[:, i, :], bank[SUM_BANK][:], -1.0 / CW,
                                                                conv_acc[:, i, :], ALU.mult, ALU.add),
                                 ln_centered)
                    else:
                        norm_scale(2, [y[:, i, :] for i in (0, 1)], OUT_NORM, y_hi[0:2], y_lo[0:2])
                    for i in range(CT):
                        dve.wait_ge(convolved, c.next(convolved))
                        src = short[:, i, :] if o == 0 else y[:, 2 + i, :]
                        link(nc.vector.scalar_tensor_tensor(y[:, 2 + i, :], src, col(BIAS_D + 2 * o + i),
                                                            bank[2 + i][:], ALU.mult, ALU.add))
                        link(nc.vector.tensor_tensor(y[:, 2 + i, :], y[:, 2 + i, :],
                                                     short[:, 2 * (o + 1) + i, :], ALU.mult))

                norm(2, [y[:, i, :] for i in (2, 3)], OUT_NORM + 2, y_hi[2:4],
                     y_lo[2:4])
                for h in range(4):
                    link(nc.vector.tensor_copy(mla_k[V_DIM:QK, h, :], key_rope[V_DIM:QK, :]))
                with c.loop(2, {"dve_step": 24, "q_ready": 4, "q_roped": 4, "scores_ready": 16,
                                "shift_ready": 16, "probs_ready": 16, "probs_scaled": 16,
                                "mixed_ready": 4, "mixed_copied": 4}) as g:
                    for h in range(4):
                        dve.wait_ge(q_ready, c.next(q_ready))
                        nc.vector.tensor_tensor(rope_a[V_DIM:QK, :], bank[h][V_DIM:QK, :],
                                                trig[V_DIM:QK, :], ALU.mult)
                        link(nc.vector.tensor_tensor(rope_b[V_DIM:QK, :], bank[h][QK:P, :], trig[QK:P, :],
                                                     ALU.mult))
                        link(nc.vector.tensor_tensor(mla_q[V_DIM:QK, h, :], rope_a[V_DIM:QK, :],
                                                     rope_b[V_DIM:QK, :], ALU.add), q_roped)

                    def maxima(h):
                        for t in range(TT):
                            dve.wait_ge(scores_ready, c.next(scores_ready))
                            link(nc.vector.reduce_max(row_max[:, t:t + 1], bank[t][:], AX_X))
                            link(nc.vector.tensor_scalar(row_shift[:, t:t + 1], row_max[:, t:t + 1],
                                                         -QK ** -0.5, None, ALU.mult), shift_ready)

                    def over_sums(h):
                        dve.wait_ge(probs_ready, c.next(probs_ready, TT))
                        link(nc.vector.reciprocal(row_inv[:], row_sum[:]))
                        for t in range(TT):
                            nc.vector.tensor_scalar(probs[:, h % 2, t, :], probs[:, h % 2, t, :],
                                                    row_inv[:, t:t + 1], None, ALU.mult
                                                    ).then_inc(probs_scaled, c.add(probs_scaled))
                        dve.wait_ge(probs_scaled, c.at(probs_scaled))

                    maxima(0)
                    over_sums(0)
                    for h in range(4):
                        if h < 3:
                            maxima(h + 1)
                            over_sums(h + 1)
                        dve.wait_ge(mixed_ready, c.next(mixed_ready))
                        out = y[(h % 2) * V_DIM:(h % 2 + 1) * V_DIM, bass.ds(2 * g + (4 + h // 2), 1), :]
                        link(nc.vector.tensor_copy(out.rearrange("p a n -> p (a n)"), bank[7][0:V_DIM, :]),
                             mixed_copied)
                norm(4, [y[:, 4 + i, :] for i in range(4)], OUT_NORM + 4, y_hi[4:8],
                     y_lo[4:8])
                absorb(stage + 1, 1.0)

            def add_outputs(total):
                for m in range(DC):
                    dve.wait_ge(acc_ready, c.next(acc_ready))
                    link(nc.vector.tensor_tensor(total[:, m, :], total[:, m, :], bank[m % 4][:], ALU.add), acc_free)

            def by_residue(v):
                return v.rearrange("p (r i) -> p i r", r=RES)

            def by_token(v):
                return v.rearrange("p (i r) -> p i r", r=RES)

            def value_tile(g, b):
                dve.wait_ge(tile_ready, c.next(tile_ready))
                link(nc.vector.tensor_tensor(by_residue(att_vt[:, g, :]), by_token(bank[b][:]), by_token(rstd[:]),
                                             ALU.mult), tile_free)
                dve.sem_inc(vt_ready, 1)

            def attention_slot(more):
                tile_no[0] = 0
                for n in range(2 * GROUPS):
                    dve.wait_ge(tile_ready, c.next(tile_ready))
                    b = bank[RING[n % len(RING)]]
                    nc.vector.tensor_tensor(rot[:, 0, :], b[:], turn2[:, 0, :], ALU.mult)
                    nc.vector.tensor_tensor(rot[0:64, 1, :], b[64:P, :], turn2[64:P, 1, :], ALU.mult)
                    link(nc.vector.tensor_tensor(rot[64:P, 1, :], b[0:64, :], turn2[0:64, 1, :], ALU.mult),
                         tile_free)
                    link(nc.vector.tensor_tensor(by_residue(att_qk[:, n, :]), by_token(rot[:, 0, :]),
                                                 by_token(rot[:, 1, :]), ALU.add), qk_ready)

                def shift(r):
                    dve.wait_ge(soft_in, c.next(soft_in))
                    w = soft[:, r % 2, :]
                    link(nc.vector.scalar_tensor_tensor(w[:, 0:T], bank[r % 2][:], HD ** -0.5, mask[:, r, 0:T],
                                                        ALU.mult, ALU.add))
                    link(nc.vector.scalar_tensor_tensor(w[:, T:T + 2 * P], bank[2 + r % 2][:, 0:2 * P], HD ** -0.5,
                                                        mask[:, r, T:T + 2 * P], ALU.mult, ALU.add))
                    link(nc.vector.reduce_max(soft_max[:, r % 2:r % 2 + 1], w, AX_X))
                    link(nc.vector.tensor_scalar(soft_shift[:, r % 2:r % 2 + 1], soft_max[:, r % 2:r % 2 + 1],
                                                 -1.0, None, ALU.mult), soft_shifted)

                def over_sum(r):
                    dve.wait_ge(soft_exp, c.next(soft_exp))
                    link(nc.vector.reciprocal(soft_max[:, r % 2:r % 2 + 1], soft_sum[:, r % 2:r % 2 + 1]))
                    link(nc.vector.tensor_scalar(soft[:, r % 2, :], soft[:, r % 2, :],
                                                 soft_max[:, r % 2:r % 2 + 1], None, ALU.mult), soft_ready)

                shift(0)
                over_sum(0)
                for r in range(RES):
                    if r + 1 < RES:
                        shift(r + 1)
                    if r + 1 < RES:
                        over_sum(r + 1)
                    if more and r < GROUPS:
                        value_tile(r, SUM_BANK)
                dve.wait_ge(att_rounded, c.next(att_rounded))
                link(nc.vector.tensor_tensor(by_token(att_lo[:]), by_residue(bank[7][:]),
                                             by_token(att_hi[:].bitcast(F32)), ALU.subtract), att_split)
                add_outputs(att_sum)

            def z_tiles():
                for b in Z_BANKS:
                    dve.wait_ge(tile_ready, c.next(tile_ready))
                    link(nc.vector.tensor_tensor(z_in[:], bank[b][:], rstd[:], ALU.mult), tile_free)
                    dve.sem_inc(z_scaled, 1)
                    dve.wait_ge(z_out, c.next(z_out))

            def ssm_group(g, more):
                link(nc.vector.tensor_copy(gcols[:], cols2[:, bass.ds(g * GROUP_COLS, GROUP_COLS)]))
                link(nc.vector.tensor_copy(dt_g[:], dt_time[:, :, :, bass.ds(g * SH, SH)]), group_dt)
                tile_no[0] = 0
                link(nc.vector.memset(xbc_pad[:, :, 0:SSM_TAPS - 1], 0.0))
                for i in SSM_ORDER:
                    tile_out(xbc_pad[:, i, SSM_TAPS - 1:])
                    w = G_CONV_W + i * SSM_TAPS
                    link(nc.vector.tensor_scalar(xbc[:, i, :], xbc_pad[:, i, 0:T], gcols[:, w:w + 1],
                                                 gcols[:, G_CONV_B + i:G_CONV_B + i + 1], ALU.mult, ALU.add))
                    for j in range(1, SSM_TAPS):
                        last = nc.vector.scalar_tensor_tensor(xbc[:, i, :], xbc_pad[:, i, j:j + T],
                                                              gcols[:, w + j:w + j + 1], xbc[:, i, :],
                                                              ALU.mult, ALU.add)
                        link(last, conv_in if j == SSM_TAPS - 1 else dve_step)
                dve.wait_ge(sums_ready, c.next(sums_ready))
                link(nc.vector.tensor_copy(a_cum[:].rearrange("p a c h -> p (a c h)"), bank[5][:, 0:2 * CH * SH]))
                link(nc.vector.tensor_scalar(a_own[:], a_cum[:, 0], -1.0, None, ALU.mult))
                link(nc.vector.tensor_tensor(a_gap[:], a_cum[:, 1], a_cum[:, 0], ALU.subtract), gap_ready)
                dve.wait_ge(left_ready, c.next(left_ready, 2))
                for ch in range(CH):
                    dve.wait_ge(x_turned, c.next(x_turned))
                    heads = lambda v: v.rearrange("p (h n) -> p h n", h=SH)
                    wide = lambda v: v.unsqueeze(2).broadcast_to([P, SH, 64])
                    nc.vector.tensor_tensor(heads(x_time[:, ch, :]), heads(bank[ch % 2][:]),
                                            wide(dt_g[:, 0, ch, :]), ALU.mult).then_inc(x_timed, c.add(x_timed))
                    if ch:
                        dve.wait_ge(x_timed, c.at(x_timed) - 1)
                        nc.vector.tensor_tensor(heads(x_left[:, ch - 1, :]), heads(x_time[:, ch - 1, :]),
                                                wide(a_left[:, ch - 1, :]), ALU.mult
                                                ).then_inc(x_decayed, c.add(x_decayed))
                dve.wait_ge(cb_ready, c.next(cb_ready))
                link(nc.vector.tensor_tensor(cb[:].rearrange("p (c l) -> p c l", c=CH),
                                             bank[3][:].rearrange("p (c l) -> p c l", c=CH),
                                             tri[:].unsqueeze(1).broadcast_to([P, CH, P]), ALU.mult), cb_masked)
                dve.wait_ge(state_in, c.next(state_in, CH - 1))
                link(nc.vector.tensor_copy(state[:, 0, :], bank[5][:]))
                for ch in range(1, CH - 1):
                    link(nc.vector.tensor_tensor(heads(state[:, ch, :]), heads(state[:, ch - 1, :]),
                                                 wide(a_whole[:, ch, :]), ALU.mult))
                    link(nc.vector.tensor_tensor(state[:, ch, :], state[:, ch, :], bank[5 + ch][:], ALU.add),
                         state_done if ch == CH - 2 else dve_step)

                def reach_of(pair):
                    dve.wait_ge(spread_ready, c.next(spread_ready))
                    for b in range(2):
                        h, at = 2 * pair + b, 2 * (pair % 2) + b
                        src = bank[((0, 1), (6, 7))[pair % 2][b]]
                        own = a_cum[:, 0, :, h:h + 1].broadcast_to([P, CH, P])
                        nc.vector.tensor_tensor(reach[:, at, :].rearrange("p (c l) -> p c l", c=CH),
                                                src[:].rearrange("p (c l) -> p c l", c=CH), own, ALU.min
                                                ).then_inc(reach_in, c.add(reach_in))

                def reach_end(pair):
                    for b in range(2):
                        at = 2 * (pair % 2) + b
                        dve.wait_ge(reach_exp, c.next(reach_exp))
                        nc.vector.tensor_tensor(reach[:, at, :], reach[:, at, :], cb[:], ALU.mult
                                                ).then_inc(reach_done, c.add(reach_done))

                reach_of(0)
                reach_end(0)
                for pair in range(4):
                    if pair + 1 < 4:
                        reach_of(pair + 1)
                    dve.wait_ge(y_parts, c.next(y_parts))
                    out = xbc[:, pair, :]
                    nc.vector.scalar_tensor_tensor(out, out, gcols[:, G_SKIP + pair:G_SKIP + pair + 1],
                                                   bank[3][:], ALU.mult, ALU.add)
                    link(nc.vector.tensor_tensor(z_in[:, P:T], bank[5][:, P:T], scaled2[:, pair % 2, P:T], ALU.mult),
                         y_taken)
                    if pair + 1 < 4:
                        reach_end(pair + 1)
                    link(nc.vector.tensor_tensor(out[:, P:T], out[:, P:T], z_in[:, P:T], ALU.add))
                    link(nc.vector.tensor_tensor(out, out, z_act[:, pair, :], ALU.mult), y_gated)
                    if pair:
                        dve.wait_ge(norm_squared, c.next(norm_squared, 2 if pair == 1 else 1))
                        link(nc.vector.tensor_tensor(square_sum[:], square[:, 0, :] if pair == 1 else square_sum[:],
                                                     square[:, pair, :], ALU.add))
                dve.sem_inc(norm_summed, 1)
                norm_scale(4, [xbc[:, i, :] for i in range(4)], G_NORM, [ssm_hi[:, i, :] for i in range(4)],
                     [ssm_lo[:, i, :] for i in range(4)], gain=gcols, out=rms2, via=scaled2)
                if more:
                    z_tiles()
                add_outputs(ssm_sum)

            def second_mixer():
                reciprocal_rms()
                dve.wait_ge(two_loaded, c.next(two_loaded, 64))
                heads = slice(0, SG * SH)
                dve.wait_ge(tile_ready, c.next(tile_ready))
                link(nc.vector.tensor_tensor(dt_rows[:, 0, :], bank[RING[-1]][heads, :], rstd[heads, :], ALU.mult),
                     tile_free)
                link(nc.vector.tensor_scalar(dt_rows[:, 0, :], dt_rows[:, 0, :], cols2[heads, DT_COLS:DT_COLS + 1],
                                             None, ALU.add), dt_raw)
                for n in range(2):
                    link(nc.vector.tensor_tensor(turn2[:, n, :], turn2[:, n, :], rstd[:], ALU.mult))
                for g in range(GROUPS):
                    value_tile(g, RING[g])
                e, u, log, spare = (dt_rows[:, n, :] for n in (1, 2, 3, 4))
                dve.wait_ge(dt_magnitude, c.next(dt_magnitude))
                link(nc.vector.tensor_scalar(u, e, 1.0, None, ALU.add), dt_log)
                dve.wait_ge(dt_magnitude, c.next(dt_magnitude))
                link(nc.vector.tensor_scalar(spare, u, 1.0, None, ALU.subtract))
                link(nc.vector.tensor_tensor(e, e, spare, ALU.subtract))
                link(nc.vector.reciprocal(u, u))
                link(nc.vector.tensor_tensor(e, e, u, ALU.mult))
                link(nc.vector.tensor_tensor(log, log, e, ALU.add))
                link(nc.vector.scalar_tensor_tensor(dt_rows[:, 0, :], dt_rows[:, 0, :], 0.0, log, ALU.max, ALU.add),
                     dt_done)
                link(nc.vector.tensor_scalar(dt_rows[:, 1, :], dt_rows[:, 0, :], a_exp[:], -1.0, ALU.mult, ALU.mult),
                     dt_done)
                link(nc.vector.memset(att_sum[:], 0.0))
                with c.loop(3, SLOT_STEPS["dve"]):
                    attention_slot(True)
                attention_slot(False)
                link(nc.vector.memset(ssm_sum[:], 0.0))
                dve.wait_ge(dt_timed, c.next(dt_timed))
                z_tiles()
                with c.loop(SG - 1, GROUP_STEPS["dve"]) as g:
                    ssm_group(g, True)
                ssm_group(SG - 1, False)
                def merge(m, banks, free):
                    at = lambda v: v[:, bass.ds(m, 1), :].rearrange("p a n -> p (a n)")
                    dve.wait_ge(gate_ready, c.next(gate_ready))
                    link(nc.vector.tensor_tensor(gate_a[:, 0, :], banks[0][:], rstd[:], ALU.mult), gate_logit)
                    dve.wait_ge(up_ready, c.next(up_ready))
                    link(nc.vector.tensor_tensor(gate_a[:, 1, :], banks[1][:], rstd[:], ALU.mult), gate_logit)
                    if free:
                        dve.sem_inc(pair_free, c.add(pair_free))
                    dve.wait_ge(gate_open, c.next(gate_open, 2))
                    for way, total in enumerate((ssm_sum, att_sum)):
                        link(nc.vector.tensor_tensor(gate_b[:, way, :], gate_b[:, way, :], at(total), ALU.mult))
                    link(nc.vector.tensor_tensor(merged[:], gate_b[:, 0, :], gate_b[:, 1, :], ALU.add),
                         merged_ready)
                    dve.wait_ge(merged_rounded, c.next(merged_rounded))
                    link(nc.vector.tensor_tensor(at(merged_lo), merged[:], at(merged_hi).bitcast(F32),
                                                 ALU.subtract), merged_split)

                for m in range(2):
                    merge(m, [bank[b] for b in Z_BANKS[2 * m:2 * m + 2]], False)
                with c.loop(DC // 2 - 1, {"gate_ready": 2, "up_ready": 2, "gate_logit": 4, "gate_open": 4,
                                          "pair_free": 2, "dve_step": 4, "merged_ready": 2,
                                          "merged_rounded": 2, "merged_split": 2}) as i:
                    for b in range(2):
                        merge(2 * i + (2 + b), bank[2 * b:2 * b + 2], True)
                absorb(7, 1.0)

            c.add(pair_free, 2)
            dve.sem_inc(acc_free, 4)
            c.add(acc_free, 4)
            dve.sem_inc(tile_free, len(RING))
            c.add(tile_free, len(RING))
            dve.sem_inc(spec_free, 2)
            dve.wait_ge(gains_loaded, 16)
            dve.wait_ge(x_loaded, 16)
            for half in range(2):
                for b in range(4):
                    rest(4 * half + b, 0)
                add_squares(range(4 * half, 4 * half + 4))
            dve.wait_ge(consts_loaded, 16 * 3)
            rows = slice(V_DIM, P)
            link(nc.vector.tensor_copy(trig[rows, :], positions[rows, :]))
            link(nc.vector.tensor_scalar(trig_tmp[rows, :], trig[rows, :], rope_cols[rows, 0:1], None, ALU.mult))
            reduce_angle(trig_tmp[rows, :], trig[rows, :])
            link(nc.vector.tensor_scalar(trig_tmp[rows, :], trig_tmp[rows, :], rope_cols[rows, 1:2], None, ALU.add))
            reduce_angle(trig_tmp[rows, :], trig[rows, :])
            link(nc.vector.tensor_scalar(trig_tmp[rows, :], trig_tmp[rows, :], PI_MAX, -PI_MAX, ALU.min, ALU.max),
                 trig_angle)
            dve.wait_ge(trig_sine, 1)
            with c.loop(LAYERS, LAYER_STEPS["dve"]) as l:
                ffn(l * 3)
                mixer(l * 3 + 1)
                ffn(l * 3 + 2)
            reciprocal_rms()
            for half in range(2):
                for b in range(4):
                    m = 4 * half + b
                    g = gains[:, 9 * DC + m:9 * DC + m + 1]
                    link(nc.vector.scalar_tensor_tensor(x[:, m, :], x[:, m, :], g, rstd[:], ALU.mult, ALU.mult),
                         x_updated)
                    if b:
                        rest(m - 1, 6)
                rest(m, 6)
                add_squares(range(4 * half, 4 * half + 4))
            second_mixer()
            ffn(7, 1.0)
            reciprocal_rms()
            for m in range(DC):
                g = gains[:, 8 * DC + m:8 * DC + m + 1]
                link(nc.vector.scalar_tensor_tensor(x[:, m, :], x[:, m, :], g, rstd[:], ALU.mult, ALU.mult),
                     y_ready)



def tiles_of(w):
    k, m = w.shape
    return w.reshape(k // P, P, m // P, P).transpose(0, 2, 1, 3)


def block_of(tiles):
    tiles = list(tiles)
    tiles += [np.zeros((P, P), np.float32)] * (BLOCK - len(tiles))
    return np.stack(tiles, 1).reshape(P, BLOCK * P)


def down_blocks(w):
    t = tiles_of(w)
    return [block_of(t[k + a, 4 * half + m] for a in range(2) for m in range(4))
            for half in range(2) for k in range(0, t.shape[0], 2)]


def width_blocks(w):
    t = tiles_of(w)
    return [block_of(t[:, m]) for m in range(t.shape[1])]


def ffn_blocks(w_gate, w_up, w_down):
    pairs = zip(width_blocks(w_gate), width_blocks(w_up))
    return [b for pair in pairs for b in pair] + down_blocks(w_down)


def columns(v):
    return v.reshape(-1, P).T


def swapped(w):
    half = ROPE // 2
    return np.concatenate([w, w[:, half:], w[:, :half]], 1)


def mixer_blocks(w_in, w_qb, w_kvb, w_out):
    q, kv, kpe, conv, hy = np.split(w_in, np.cumsum([256, 128, 32, 512]), 1)
    t = width_blocks(conv)
    out = width_blocks(kv) + width_blocks(q)
    out += width_blocks(np.concatenate([np.zeros((D, NOPE), np.float32), swapped(kpe)], 1))
    out += [t[0], t[2], t[1], t[3]] + width_blocks(hy)
    qb = w_qb.reshape(2, P, HEADS, QK)
    kvb = w_kvb.reshape(P, HEADS, NOPE + V_DIM)
    for g in range(2):
        heads = range(4 * g, 4 * g + 4)
        out.append(block_of(np.concatenate([qb[k, :, h, :NOPE], swapped(qb[k, :, h, NOPE:])], 1)
                            for h in heads for k in range(2)))
        flat = kvb[:, 4 * g:4 * g + 4].transpose(1, 0, 2)
        keys = np.concatenate(list(flat[:, :, :NOPE]), 1)
        values = np.concatenate(list(flat[:, :, NOPE:]), 1)
        out.append(block_of([keys[:, :P], keys[:, P:], values[:, :P], values[:, P:]]))
    return out + down_blocks(np.concatenate([w_out[512:], w_out[:512]]))


def layer_columns(i):
    cols = np.zeros((LAYERS, P, LAYER_COLS), np.float32)
    for l in range(LAYERS):
        def put(at, *parts):
            for part in parts:
                cols[l, :part.shape[0], at:at + part.shape[1]] = part
                at += part.shape[1]
        put(Q_NORM, columns(i["mla_q_norm"][l]))
        put(KV_NORM, columns(i["mla_kv_norm"][l]))
        put(CONV_W, *(i["conv_dw_w"][l].T.reshape(CT, P, TAPS)))
        put(CONV_B, columns(i["conv_dw_b"][l]))
        put(LN_G, columns(i["conv_ln_g"][l]))
        put(LN_B, columns(i["conv_ln_b"][l]))
        put(SHORT_W, *(i["hy_short_w"][l].T.reshape(3 * CT, P, SHORT)))
        put(SHORT_B, columns(i["hy_short_b"][l]))
        put(FILT_B, *(i[f"hy_filt_b{n}"][l][:, None] for n in (1, 2, 3)))
        put(FILT_FREQ, i["hy_filt_freq"][l][:, None])
        put(BIAS_D, columns(i["hy_bias_d"][l].reshape(-1)))
        put(OUT_NORM, columns(np.concatenate([i["out_norm"][l][512:], i["out_norm"][l][:512]])))
    return cols


def rope_columns():
    half = ROPE // 2
    inv = (1.0 / (np.float32(10000.0) ** (np.arange(0, ROPE, 2, dtype=np.float32) / np.float32(ROPE))))
    out = np.zeros((P, 2), np.float32)
    for p in range(NOPE, P):
        out[p, 0] = inv[p % half]
        out[p, 1] = np.pi / 2 if p < QK else np.pi if p < QK + half else 0.0
    return out


def filter_positions():
    t = np.linspace(0.0, 1.0, T, dtype=np.float32)[:, None]
    bands = (EMB - 1) // 2
    ang = (2.0 * np.pi * np.arange(T, dtype=np.float32)[:, None] / T).astype(np.float32)
    fb = np.linspace(1e-4, bands - 1, bands, dtype=np.float32)[None]
    z = np.concatenate([t, np.cos(fb * ang), -np.sin(fb * ang)], 1).astype(np.float32)
    deltas = np.linspace(np.log(1e-2) / 1.5, np.log(1e-2) / 0.3, CW, dtype=np.float32)
    decay = np.exp(-t * np.abs(deltas)).astype(np.float32)
    return np.ascontiguousarray(z.T), decay.reshape(TT, P, CW).transpose(1, 0, 2)


def transforms():
    n = np.arange(T, dtype=np.float64)
    out = []
    for shift in (0.0, 0.5):
        a = 2 * np.pi * np.outer(n + shift, n + 0.5) / (2 * T)
        m = np.stack([np.cos(a), np.sin(a)])
        out.append(m.reshape(2, TT, P, T).transpose(2, 0, 1, 3))
    return np.stack(out).astype(np.float32)


def slot_blocks(w_qkv, w_out, j):
    w = w_qkv.reshape(D, 3, 12, HD)
    heads = lambda n, j: [b for g in range(GROUPS) for b in width_blocks(w[:, n, 4 * g + j])]
    ahead = heads(2, j + 1) if j + 1 < 4 else []
    if j < 0:
        return ahead
    return heads(0, j) + heads(1, j) + ahead + [block_of(tiles_of(w_out[j * HD:(j + 1) * HD])[0])]


def z_blocks(w_z, g):
    return width_blocks(w_z[:, g * T:(g + 1) * T])


def gate_blocks(w):
    t = width_blocks(w)
    return [t[m + 8 * way] for m in range(8) for way in range(2)]


def group_blocks(w_x, w_b, w_c, w_z, w_gates, w_out, g):
    wide, narrow = slice(g * T, (g + 1) * T), slice(g * P, (g + 1) * P)
    out = width_blocks(w_b[:, narrow]) + width_blocks(w_c[:, narrow]) + width_blocks(w_x[:, wide])
    out += z_blocks(w_z, g + 1) if g + 1 < SG else gate_blocks(w_gates)[:4]
    t = tiles_of(w_out[wide])
    return out + [block_of(t[k, m + a] for a in range(2) for k in range(4)) for m in range(0, DC, 2)]


def second_blocks(i):
    z, xbc, dt, qkv, gates = np.split(i["w_in_2"][0], np.cumsum([2048, 3072, 32, 4608]), 1)
    out = width_blocks(np.concatenate([dt, np.zeros((D, P - 32), np.float32)], 1)) 
    for j in range(-1, 4):
        out += slot_blocks(qkv, i["w_att_out_2"][0], j)
    w_x, w_b, w_c = np.split(xbc, [2048, 2560], 1)
    out += z_blocks(z, 0)
    for g in range(SG):
        out += group_blocks(w_x, w_b, w_c, z, gates, i["w_ssm_out_2"][0], g)
    out += gate_blocks(gates)[4:]
    out += down_blocks(i["w_mix_out_2"][0])
    return out + ffn_blocks(i["w_ffn_gate_2"][0], i["w_ffn_up_2"][0], i["w_ffn_down_2"][0])


def second_columns(i):
    cols = np.zeros((P, SG * GROUP_COLS + 18), np.float32)
    channels = lambda v: (v[..., :2048], v[..., 2048:2560], v[..., 2560:])
    for g in range(SG):
        at = g * GROUP_COLS
        pick = lambda v: np.concatenate([part[..., g * n:(g + 1) * n] for part, n in
                                         zip(channels(v), (T, P, P))], -1)
        w = pick(i["conv_w_2"][0])
        cols[:, at + G_CONV_W:at + G_CONV_B] = w.T.reshape(SSM_TILES, P, SSM_TAPS).transpose(1, 0, 2).reshape(P, -1)
        cols[:, at + G_CONV_B:at + G_SKIP] = columns(pick(i["conv_b_2"][0]))
        cols[:, at + G_SKIP:at + G_NORM] = columns(np.repeat(i["d_skip_2"][0][g * SH:(g + 1) * SH], 64))
        cols[:, at + G_NORM:at + GROUP_COLS] = columns(i["ssm_norm_2"][0][g * T:(g + 1) * T])
    cols[:, SG * GROUP_COLS:DT_COLS] = columns(i["b_gate_2"][0])
    cols[:SG * SH, DT_COLS] = i["dt_bias_2"][0]
    cols[:SG * SH, DT_COLS + 1] = i["a_log_2"][0]
    return cols


def second_tables():
    q = np.arange(P)[:, None]
    mask = np.full((P, RES, T + 2 * P), MASKED, np.float32)
    for r in range(RES):
        tq = 4 * q + r
        for rk in range(RES):
            tk = 4 * np.arange(P)[None] + rk
            ok = (tk <= tq) & (tq - tk <= 128)
            mask[:, r, rk * P:(rk + 1) * P][ok] = 0.0
        i = np.arange(P)[None]
        mask[:, r, T:T + P][i <= q] = 0.0
        mask[:, r, T + P:][(i <= q) & ((q - i) % 4 == 0)] = 0.0
    half = HD // 2
    inv = np.float32(10000.0) ** (-np.arange(half, dtype=np.float32) / half)
    ang = (np.arange(T, dtype=np.float32)[None] * inv[:, None].astype(np.float32)).astype(np.float32)
    cos, sin = np.cos(ang), np.sin(ang)
    turn = np.stack([np.concatenate([cos, cos]), np.concatenate([sin, -sin])], 1).astype(np.float32)
    sel = np.zeros((SH, 12, P), np.float32)
    for h in range(SH):
        sel[h, h] = 1.0
        sel[h, SH + h // 2, 64 * (h % 2):64 * (h % 2 + 1)] = 1.0
    tri = np.triu(np.ones((P, P), np.float32))
    return {"mask": mask, "turn2": turn, "sel": sel.reshape(SH, 12 * P), "tri": tri}


def arrange(i):
    blocks = []
    for l in range(LAYERS):
        blocks += ffn_blocks(i["ffn1_w_gate"][l], i["ffn1_w_up"][l], i["ffn1_w_down"][l])
        blocks += mixer_blocks(i["w_in"][l], i["mla_w_qb"][l], i["mla_w_kvb"][l], i["w_out"][l])
        blocks += ffn_blocks(i["ffn2_w_gate"][l], i["ffn2_w_up"][l], i["ffn2_w_down"][l])
    blocks += second_blocks(i)
    blocks += [block_of([])] * (-len(blocks) % RAW)
    z, decay = filter_positions()
    gains = [columns(i[n][l]) for l in range(LAYERS) for n in ("ffn1_norm", "mix_norm", "ffn2_norm")]
    gains += [columns(i["norm_mix_2"][0]), columns(i["norm_ffn_2"][0]), columns(i["norm_final_2"]), columns(i["final_norm"])]
    return {
        "w": np.stack(blocks),
        "x": i["x"][0].T.reshape(DC, P, T).transpose(1, 0, 2),
        "gains": np.concatenate(gains, 1),
        "ident": np.eye(P, dtype=np.float32),
        "rope_cols": rope_columns(),
        "positions": np.broadcast_to(i["positions"][0][None], (P, T)),
        "layer_cols": layer_columns(i),
        "filt_w": np.stack([np.concatenate([np.concatenate([i["hy_filt_w1"][l], np.zeros((FILT - EMB, FILT), np.float32)]),
                                            i["hy_filt_w2"][l], i["hy_filt_w3"][l], i["hy_filt_w4"][l]], 1)
                            for l in range(LAYERS)]),
        "filt_z": z,
        "decay": decay,
        "decay_back": np.array([[0.0]] + [[1.0]] * (P - 1), np.float32),
        "dft": transforms(),
        "cols2": second_columns(i),
        **second_tables(),
    }


def kernel(**inputs):
    import concourse.bacc as _bacc
    from concourse.bass_utils import run_bass_kernel_spmd as _run

    nc = _bacc.Bacc("TRN2", target_bir_lowering=False, num_devices=1)
    arrays, io = {}, {}
    for name, a in arrange({n: np.asarray(v) for n, v in inputs.items()}).items():
        a = np.ascontiguousarray(a)
        arrays["in_" + name] = a
        io[name] = nc.dram_tensor("in_" + name, a.shape, mybir.dt.from_np(a.dtype), kind="ExternalInput").ap()
    io["out"] = nc.dram_tensor("out", (P, DC, T), F32, kind="ExternalOutput").ap()
    build(nc, io)
    out = _run(nc, [arrays], core_ids=[0]).results[0]["out"]
    return out.transpose(1, 0, 2).reshape(D, T).T[None]
```
